# Optimizing a Trainium2 kernel written in Bass

```python
import jax, jax.numpy as jnp
from jax import lax
import numpy as np

D_MODEL = 1024
BATCH = 1
SEQ = 256
DEPTH = 2

MEM_LEN = 256
EPS = 1e-6
CONV_A_WIDTH = D_MODEL // 2
CONV_A_KERNEL = 31
DIL_PATTERNS = ((128, 1), (512, 4), (2048, 16))
DIL_GROUPS = len(DIL_PATTERNS)
DIL_HEADS = 4
DIL_HEAD_DIM = 64
DIL_WIDTH = DIL_GROUPS * DIL_HEADS * DIL_HEAD_DIM
DIL_OUT = DIL_HEADS * DIL_HEAD_DIM
BLOCK = 128
SC_WIDTH = D_MODEL // 2
SC_KERNEL = 3
N_BRANCH = 3
OFF_A = 0
OFF_Q = OFF_A + 2 * CONV_A_WIDTH
OFF_K = OFF_Q + DIL_WIDTH
OFF_V = OFF_K + DIL_WIDTH
OFF_CB = OFF_V + DIL_WIDTH
OFF_CC = OFF_CB + SC_WIDTH
OFF_CH = OFF_CC + SC_WIDTH
OFF_G = OFF_CH + SC_WIDTH
N_IN = OFF_G + N_BRANCH * D_MODEL
XATTN_HEADS = 4
XATTN_HEAD_DIM = D_MODEL // XATTN_HEADS
D_FF = ((8 * D_MODEL // 3 + 255) // 256) * 256
N_EXPERTS = 8
TOP_K = 2
MOE_FF = 7 * D_MODEL // 2
N_DENSE = (DEPTH + 1) // 2
N_MOE = DEPTH // 2

kernel_name = "hybrid_conv_dilated_shortconv_moe_block"

def rms_norm(x, g):
    x32 = x.astype(jnp.float32)
    y = x32 * lax.rsqrt(jnp.mean(x32 * x32, axis=-1, keepdims=True) + EPS)
    return (y * g.astype(jnp.float32)).astype(x.dtype)

def layer_norm(x, g, b):
    x32 = x.astype(jnp.float32)
    mu = jnp.mean(x32, axis=-1, keepdims=True)
    xc = x32 - mu
    y = xc * lax.rsqrt(jnp.mean(xc * xc, axis=-1, keepdims=True) + EPS)
    return (y * g.astype(jnp.float32) + b.astype(jnp.float32)).astype(x.dtype)

def causal_depthwise_conv(u, w):
    k_width, c = w.shape
    return lax.conv_general_dilated(
        u, w.astype(u.dtype)[:, None, :], window_strides=(1,), padding=[(k_width - 1, 0)],
        dimension_numbers=("NWC", "WIO", "NWC"), feature_group_count=c)

def dilated_window_attention(q, k, v, dilation, n_steps):
    b, s, h, dh = q.shape
    span = dilation * BLOCK
    s_pad = -(-s // span) * span
    nb = s_pad // span
    pad = [(0, 0), (0, s_pad - s), (0, 0), (0, 0)]

    def blocks(t):
        return jnp.pad(t, pad).reshape(b, nb, BLOCK, dilation, h, dh)

    def band(t):
        prev = jnp.pad(t[:, :-1], [(0, 0), (1, 0), (0, 0), (0, 0), (0, 0), (0, 0)])
        return jnp.concatenate([prev, t], axis=2)

    qb = blocks(q)
    kw, vw = band(blocks(k)), band(blocks(v))
    scores = jnp.einsum('bnqrhe,bnkrhe->bnrhqk', qb, kw) * (dh ** -0.5)
    qi = jnp.arange(BLOCK)[:, None]
    kj = jnp.arange(2 * BLOCK)[None, :]
    dist = BLOCK + qi - kj
    in_band = (dist >= 0) & (dist <= n_steps)
    has_prev = jnp.arange(nb)[:, None, None] > 0
    valid = in_band[None] & (has_prev | (kj >= BLOCK)[None])
    scores = jnp.where(valid[None, :, None, None], scores, -jnp.inf)
    m = jnp.max(scores, axis=-1, keepdims=True)
    p = jnp.exp(scores - m)
    den = jnp.sum(p, axis=-1, keepdims=True)
    out = jnp.einsum('bnrhqk,bnkrhe->bnqrhe', p / den, vw)
    lse = (m + jnp.log(den))[..., 0]
    out = out.reshape(b, s_pad, h, dh)[:, :s]
    lse = lse.transpose(0, 1, 4, 2, 3).reshape(b, s_pad, h)[:, :s]
    return out, lse

def hybrid_mixer(h, w_in, b_in, a_conv_w, a_conv_b, a_ln_g, a_ln_b, a_w_out,
                 b_w_out, c_conv_w, c_w_out, w_o):
    bsz, s, _ = h.shape
    z = h @ w_in + b_in
    a = z[..., OFF_A:OFF_A + CONV_A_WIDTH] * jax.nn.sigmoid(z[..., OFF_A + CONV_A_WIDTH:OFF_Q])
    a = causal_depthwise_conv(a, a_conv_w) + a_conv_b
    y_a = jax.nn.silu(layer_norm(a, a_ln_g, a_ln_b)) @ a_w_out
    def heads(t):
        return t.reshape(bsz, s, DIL_GROUPS, DIL_HEADS, DIL_HEAD_DIM).astype(jnp.float32)
    q, k, v = heads(z[..., OFF_Q:OFF_K]), heads(z[..., OFF_K:OFF_V]), heads(z[..., OFF_V:OFF_CB])
    outs, lses = [], []
    for g, (window, dilation) in enumerate(DIL_PATTERNS):
        o, l = dilated_window_attention(q[:, :, g], k[:, :, g], v[:, :, g], dilation, window // dilation)
        outs.append(o)
        lses.append(l)
    wts = jax.nn.softmax(jnp.stack(lses, axis=0), axis=0)
    o = jnp.sum(wts[..., None] * jnp.stack(outs, axis=0), axis=0)
    y_b = o.reshape(bsz, s, DIL_OUT).astype(h.dtype) @ b_w_out
    gb, gc, hc = z[..., OFF_CB:OFF_CC], z[..., OFF_CC:OFF_CH], z[..., OFF_CH:OFF_G]
    y_c = (gb * causal_depthwise_conv(gc * hc, c_conv_w)) @ c_w_out
    gates = jax.nn.sigmoid(z[..., OFF_G:].reshape(bsz, s, N_BRANCH, D_MODEL))
    merged = gates[..., 0, :] * y_a + gates[..., 1, :] * y_b + gates[..., 2, :] * y_c
    return merged @ w_o

def memory_cross_attention(h, mem_n, wq, wk, wv, wo):
    bsz, s, _ = h.shape
    q = (h @ wq).reshape(bsz, s, XATTN_HEADS, XATTN_HEAD_DIM).astype(jnp.float32)
    k = (mem_n @ wk).reshape(bsz, -1, XATTN_HEADS, XATTN_HEAD_DIM).astype(jnp.float32)
    v = (mem_n @ wv).reshape(bsz, -1, XATTN_HEADS, XATTN_HEAD_DIM).astype(jnp.float32)
    p = jax.nn.softmax(jnp.einsum('bshe,bmhe->bhsm', q, k) * (XATTN_HEAD_DIM ** -0.5), axis=-1)
    o = jnp.einsum('bhsm,bmhe->bshe', p, v).reshape(bsz, s, D_MODEL).astype(h.dtype)
    return o @ wo

def swiglu(h, w1, w3, w2):
    return (jax.nn.silu(h @ w1) * (h @ w3)) @ w2

def moe_swiglu(h, w_router, w1, w3, w2):
    logits = (h @ w_router).astype(jnp.float32)
    top_val, top_idx = lax.top_k(logits, TOP_K)
    top_w = jax.nn.softmax(top_val, axis=-1)
    combine = jnp.sum(jax.nn.one_hot(top_idx, N_EXPERTS, dtype=jnp.float32) * top_w[..., None], axis=-2)
    out = jnp.zeros_like(h)
    for e in range(N_EXPERTS):
        out = out + combine[..., e:e + 1].astype(h.dtype) * swiglu(h, w1[e], w3[e], w2[e])
    return out

def setup_inputs(seed: int = 0) -> dict:
    key = jax.random.key(seed)
    ks = iter(jax.random.split(key, 40))

    def nrm(shape, scale):
        return jax.random.normal(next(ks), shape, jnp.float32) * scale

    def gain(shape):
        return 1.0 + nrm(shape, 0.02)

    L = DEPTH
    return {
        "x": nrm((BATCH, SEQ, D_MODEL), 1.0),
        "mem": nrm((BATCH, MEM_LEN, D_MODEL), 1.0),
        "norm_mix_g": gain((L, D_MODEL)),
        "w_in": nrm((L, D_MODEL, N_IN), D_MODEL ** -0.5),
        "b_in": nrm((L, N_IN), 0.02),
        "a_conv_w": nrm((L, CONV_A_KERNEL, CONV_A_WIDTH), CONV_A_KERNEL ** -0.5),
        "a_conv_b": nrm((L, CONV_A_WIDTH), 0.02),
        "a_ln_g": gain((L, CONV_A_WIDTH)),
        "a_ln_b": nrm((L, CONV_A_WIDTH), 0.02),
        "a_w_out": nrm((L, CONV_A_WIDTH, D_MODEL), CONV_A_WIDTH ** -0.5),
        "b_w_out": nrm((L, DIL_OUT, D_MODEL), DIL_OUT ** -0.5),
        "c_conv_w": nrm((L, SC_KERNEL, SC_WIDTH), SC_KERNEL ** -0.5),
        "c_w_out": nrm((L, SC_WIDTH, D_MODEL), SC_WIDTH ** -0.5),
        "w_o": nrm((L, D_MODEL, D_MODEL), D_MODEL ** -0.5),
        "norm_x_g": gain((L, D_MODEL)),
        "norm_mem_g": gain((L, D_MODEL)),
        "xq_w": nrm((L, D_MODEL, D_MODEL), D_MODEL ** -0.5),
        "xk_w": nrm((L, D_MODEL, D_MODEL), D_MODEL ** -0.5),
        "xv_w": nrm((L, D_MODEL, D_MODEL), D_MODEL ** -0.5),
        "xo_w": nrm((L, D_MODEL, D_MODEL), D_MODEL ** -0.5),
        "norm_ffn_g": gain((L, D_MODEL)),
        "ffn_w1": nrm((N_DENSE, D_MODEL, D_FF), D_MODEL ** -0.5),
        "ffn_w3": nrm((N_DENSE, D_MODEL, D_FF), D_MODEL ** -0.5),
        "ffn_w2": nrm((N_DENSE, D_FF, D_MODEL), D_FF ** -0.5),
        "moe_router": nrm((N_MOE, D_MODEL, N_EXPERTS), D_MODEL ** -0.5),
        "moe_w1": nrm((N_MOE, N_EXPERTS, D_MODEL, MOE_FF), D_MODEL ** -0.5),
        "moe_w3": nrm((N_MOE, N_EXPERTS, D_MODEL, MOE_FF), D_MODEL ** -0.5),
        "moe_w2": nrm((N_MOE, N_EXPERTS, MOE_FF, D_MODEL), MOE_FF ** -0.5),
        "final_g": gain((D_MODEL,)),
    }

def reference(x, mem, norm_mix_g, w_in, b_in, a_conv_w, a_conv_b, a_ln_g, a_ln_b, a_w_out,
              b_w_out, c_conv_w, c_w_out, w_o, norm_x_g, norm_mem_g, xq_w, xk_w, xv_w, xo_w,
              norm_ffn_g, ffn_w1, ffn_w3, ffn_w2, moe_router, moe_w1, moe_w3, moe_w2, final_g):
    for layer in range(DEPTH):
        h = rms_norm(x, norm_mix_g[layer])
        x = x + hybrid_mixer(h, w_in[layer], b_in[layer], a_conv_w[layer], a_conv_b[layer],
                             a_ln_g[layer], a_ln_b[layer], a_w_out[layer], b_w_out[layer],
                             c_conv_w[layer], c_w_out[layer], w_o[layer])
        h = rms_norm(x, norm_x_g[layer])
        mem_n = rms_norm(mem, norm_mem_g[layer])
        x = x + memory_cross_attention(h, mem_n, xq_w[layer], xk_w[layer], xv_w[layer], xo_w[layer])
        h = rms_norm(x, norm_ffn_g[layer])
        if layer % 2 == 0:
            i = layer // 2
            x = x + swiglu(h, ffn_w1[i], ffn_w3[i], ffn_w2[i])
        else:
            i = layer // 2
            x = x + moe_swiglu(h, moe_router[i], moe_w1[i], moe_w3[i], moe_w2[i])
    return rms_norm(x, final_g)


_drawn_inputs = setup_inputs


def setup_inputs(seed=0):
    import zlib

    import numpy as np

    out = dict(_drawn_inputs(seed))
    spreads = {}
    factors = {'a_ln_b': 2.807,
     'norm_x_g': 5.042,
     'norm_mem_g': 4.225,
     'final_g': 7.495,
     'norm_ffn_g': 3.41}
    for name, (base, spread) in spreads.items():
        noise = np.random.default_rng([zlib.crc32(name.encode()), seed]).standard_normal(out[name].shape)
        drawn = base * np.exp(spread * noise) if base else spread * noise
        out[name] = __import__('jax').numpy.asarray(drawn.astype(out[name].dtype))
    for name, factor in factors.items():
        out[name] = (out[name] * factor).astype(out[name].dtype)
    return out
```

```python
import concourse.bass as bass
from concourse import mybir
from contextlib import ExitStack

F32 = mybir.dt.float32
F32R = mybir.dt.float32r
BF16 = mybir.dt.bfloat16
U32 = mybir.dt.uint32
I32 = mybir.dt.int32
ALU = mybir.AluOpType
ACT = mybir.ActivationFunctionType
AX = mybir.AxisListType

P = 128
D = 1024
S = 256
DB = D // P
TB = S // P
EPS = 1e-6
LAYERS = 2
AW = 512
AB = AW // P
KA, KC = 31, 3
GROUPS, HEADS, DH = 3, 4, 64
XH = 4
FF = 2816
FFB = FF // 256
NE, EFF = 8, 3584
FSTEPS = EFF // 512
SLOTS = 128
RAW, SPLIT = 6, 3
CW = 2048
NEG = -1e30

IN_BLOCKS = [2, 0, 3, 1, 13, 14, 15, 17, 16, 18, 4, 5, 6, 7, 8, 9, 10, 11, 12]
C_AGATE, C_C, C_QKV, C_COUT, C_GC, C_AOUT, C_GA, C_BOUT, C_GB, C_WO, C_XK, C_XQ, C_XV, C_XO, C_FFN = (
    0, 4, 10, 19, 21, 25, 27, 31, 33, 37, 41, 45, 49, 53, 57)
BASE = [0, 57 + 3 * FFB]
MOE = BASE[1] + 57
PER_E = 6 * FSTEPS
GA_BLOCK, GB_BLOCK, GC_BLOCK = 19, 23, 27
HEAD_AT = [16, 19, 22, 25]
OT_AT = 29
G_MIX, G_X, G_MEM, G_FFN, G_FIN, A_CB, A_LG, A_LB, C_CW = 0, 16, 32, 48, 64, 72, 80, 88, 96


def trunk(nc, x, mem, norm_mix_g, w_in, b_in, a_conv_w, a_conv_b, a_ln_g, a_ln_b, a_w_out, b_w_out,
          c_conv_w, c_w_out, w_o, norm_x_g, norm_mem_g, xq_w, xk_w, xv_w, xo_w, norm_ffn_g, ffn_w1,
          ffn_w3, ffn_w2, moe_router, moe_w1, moe_w3, moe_w2, final_g, out):
    with ExitStack() as ctx:
        def sb(name, shape, dt=F32):
            return ctx.enter_context(nc.sbuf_tensor(name, shape, dt))

        def sem(name):
            return ctx.enter_context(nc.semaphore(name))

        raw = sb("raw", [P, RAW, CW])
        whi = sb("whi", [P, SPLIT, CW], F32R)
        wlo = sb("wlo", [P, SPLIT, CW], F32R)
        h_hl = sb("h_hl", [P, 2, DB, S], F32R)
        act_hl = sb("act_hl", [P, 4096], F32R)
        xT = sb("xT", [P, DB, S])
        memhat = sb("memhat", [P, DB, S])
        U = sb("U", [P, 14720])
        par = sb("par", [P, 4, P])
        ident = sb("ident", [P, P])
        ones = sb("ones", [P, P])
        mask = sb("mask", [P, GROUPS, S], BF16)
        rstd = sb("rstd", [P, S])
        router = sb("router", [P, DB, NE])
        small = sb("small", [P, 32])
        bank = [ctx.enter_context(nc.psum_tensor(f"bank{i}", [P, 512], F32)) for i in range(8)]

        def u(at, *shape):
            size = 1
            for s_ in shape:
                size *= s_
            ap = U[:, at:at + size]
            if len(shape) == 2:
                return ap.rearrange("p (a b) -> p a b", a=shape[0])
            if len(shape) == 3:
                return ap.rearrange("p (a b c) -> p a b c", a=shape[0], b=shape[1])
            return ap

        def v(at, *shape):
            size = 1
            for s_ in shape:
                size *= s_
            ap = act_hl[:, at:at + size]
            return ap.rearrange("p (a b) -> p a b", a=shape[0]) if len(shape) == 2 else ap

        sq, hf = u(0, DB, S), u(2048, DB, S)
        qT, kT = u(0, 6, S), u(1536, 6, S)
        vtok = u(3072, TB, GROUPS * HEADS * DH)
        apad = u(4608, AB, KA - 1 + S)
        sg = u(4608, 2, 2, S)
        aacc, agate = u(5752, AB, S), u(5752, AB, S)
        cb = u(6776, AB, S)
        cpad = u(7800, AB, KC - 1 + S)
        cacc, ccv, asq = u(8832, AB, S), u(8832, AB, S), u(8832, AB, S)
        Y = u(6776, DB, S)
        prob0, prob1 = u(9856, GROUPS, P), u(9856 + 384, GROUPS, S)
        pT0, pT1 = u(11008, GROUPS, P), u(11008 + 384, GROUPS, S)
        otok = u(12160, TB, HEADS * DH)
        merged = u(12672, DB, S)
        vbias = u(12672, GROUPS * HEADS * DH)
        c_hi, c_lo = v(0, AB, S), v(1024, AB, S)
        a_hi, a_lo = v(2048, AB, S), v(3072, AB, S)
        o_hi, o_lo = v(0, 2, S), v(512, 2, S)
        kx, qx = u(4096, DB, S), u(6144, DB, S)
        vx = u(8192, TB, D)
        probx = u(10240, XH * TB, S)
        pTx = u(12288, XH * TB, S)
        m_hi, m_lo = v(0, DB, S), v(2048, DB, S)
        sil, gf = u(4096, 2, 512), u(5120, 2, 512)
        zerosf = u(6144, 256)
        zeros = zerosf.bitcast(BF16)
        y0 = U[:, 12800:13056].bitcast(BF16)
        g_hi, g_lo = v(0, 2, 512), v(1024, 2, 512)
        htok = u(4096, TB, D)
        sel = u(6144, TB, NE + 1, SLOTS)
        wsel = u(8448, TB, NE, SLOTS)
        esil, eg = u(8448, 2, 512), u(9472, 512)
        wselT = u(10496, NE + 1, S)
        y = u(12800, D)
        rt = U[:, 13824:14720]
        iota = rt[:, 0:128]
        strict = rt[:, 128:256]
        allone = rt[:, 256:384]
        lg, top, idxf, oh0, oh1, msk, comb, posm, posr = (
            rt[:, 448 + 16 * i:464 + 16 * i].rearrange("p (b e) -> p b e", e=NE) for i in range(9))
        idxu = sb("idxu", [P, TB, NE], U32)
        wts = rt[:, 592:608]
        cntf = rt[:, 608:609]
        iota8 = rt[:, 616:624]
        cntu = sb("cntu", [P, 1], U32)
        eT_hi, eT_lo = v(0, 512), v(512, 512)
        he_hi, he_lo = v(2048, D), v(3072, D)
        xin, min_ = u(4096, TB, D), u(6144, TB, D)
        prow = u(8192, 4, P)
        dist = U[:, 8704:8960].bitcast(I32)
        rest = U[:, 8960:9216].bitcast(I32)
        ban = u(9216, 2, S)
        yout = u(4096, TB, D)

        w_raw = [sem(f"w_raw{i}") for i in range(RAW)]
        hi_ready = sem("hi_ready")
        lo_ready = sem("lo_ready")
        w_used = sem("w_used")
        in_par, in_x, in_mem, in_vb, in_rt = (sem(s_) for s_ in ("in_par", "in_x", "in_mem", "in_vb", "in_rt"))
        const = sem("const")
        rt_const = sem("rt_const")
        tr_done = sem("tr_done")
        par_ready = sem("par_ready")
        x_ready = sem("x_ready")
        mT_ready = sem("mT_ready")
        sq_ready = sem("sq_ready")
        ss_done = sem("ss_done")
        ms_ready = sem("ms_ready")
        rt_ready = sem("rt_ready")
        hf_ready = sem("hf_ready")
        h_hi_s = sem("h_hi_s")
        h_lo_s = sem("h_lo_s")
        mf_ready, m_hi_s, m_lo_s = sem("mf_ready"), sem("m_hi_s"), sem("m_lo_s")
        out_act = sem("out_act")
        out_dve = sem("out_dve")
        gated = sem("gated")
        pads = sem("pads")
        conv_a, conv_c = sem("conv_a"), sem("conv_c")
        c_f, c_hi_s, c_lo_s = sem("c_f"), sem("c_hi_s"), sem("c_lo_s")
        ln_st = sem("ln_st")
        ln_xc, ln_sq, ln_var, ln_rt, ln_y = (sem(s_) for s_ in ("ln_xc", "ln_sq", "ln_var", "ln_rt", "ln_y"))
        a_f, a_hi_s, a_lo_s = sem("a_f"), sem("a_hi_s"), sem("a_lo_s")
        sc_done, mx_ready, pr_ready, pt_done, pT_ready, pv_done, o_ready = (
            sem(s_) for s_ in ("sc_done", "mx_ready", "pr_ready", "pt_done", "pT_ready", "pv_done", "o_ready"))
        oT_done, o_hi_s, o_lo_s = sem("oT_done"), sem("o_hi_s"), sem("o_lo_s")
        mg_hi_s, mg_lo_s = sem("mg_hi_s"), sem("mg_lo_s")
        xs_done, xm_ready, xp_ready, xn_ready, xpt_done, xpT_ready, xpv_done, xo_hi_s, xo_lo_s = (
            sem(s_) for s_ in ("xs_done", "xm_ready", "xp_ready", "xn_ready", "xpt_done", "xpT_ready",
                               "xpv_done", "xo_hi_s", "xo_lo_s"))
        z_ready = sem("z_ready")
        silu_s, g_s, g_hi_s, g_lo_s = sem("silu_s"), sem("g_s"), sem("g_hi_s"), sem("g_lo_s")
        rl_done, ht_done, ht_ready, rl_ready, re_ready, route = (
            sem(s_) for s_ in ("rl_done", "ht_done", "ht_ready", "rl_ready", "re_ready", "route"))
        mk_ready, cnt_done, count_ready, sel_ready, wt_done, wt_ready = (
            sem(s_) for s_ in ("mk_ready", "cnt_done", "count_ready", "sel_ready", "wt_done", "wt_ready"))
        y_zero, ga_done, he_hi_s, he_lo_s, e_silu, e_g, e_tr, e_hi, e_lo, y_ev, y_sc, y_add = (
            sem(s_) for s_ in ("y_zero", "ga_done", "he_hi_s", "he_lo_s", "e_silu", "e_g", "e_tr", "e_hi",
                               "e_lo", "y_ev", "y_sc", "y_add"))
        fo_done, fo_ready, fo_act, out_sent = (
            sem(s_) for s_ in ("fo_done", "fo_ready", "fo_act", "out_sent"))
        dve_own = sem("dve_own")
        round_own = sem("round_own")

        block = ctx.enter_context(nc.Block())

        def local(n):
            lay = int(n >= BASE[1])
            return lay, n - BASE[lay]

        def by_vector(n):
            c = local(n)[1]
            return c in (1, 3, 7, 9, 16, 17, 18)

        def to_residual(c):
            return C_WO <= c < C_XK or C_XO <= c < C_FFN

        def taken(n):
            lay, c = local(n)
            if to_residual(c):
                return x_ready, 12 * lay + (4 + c - C_WO if c < C_XK else 8 + c - C_XO) + 1
            dense = [BASE[i] + k for i in range(LAYERS) for k in range(C_FFN) if not to_residual(k)]
            mine = by_vector(n)
            return (out_dve if mine else out_act), sum(1 for m in dense if m <= n and by_vector(m) == mine)

        def ln_bank(n):
            return 2 * (n % 2) + 1

        @block.sync
        def _(sp):
            def load(slot, value, dst_words, pattern, src, wait=None):
                if wait is not None:
                    sp.wait_ge(lo_ready, wait)
                sp.dma_start(raw[:, slot, 0:dst_words].rearrange(pattern[0], **pattern[1]), src)\
                  .then_inc(w_raw[slot], 16)

            def k8(w, block_):
                return w.rearrange("(k p) n -> p k n", p=P)[:, :, 256 * block_:256 * block_ + 256]

            def dense(n, src, k):
                load(n % RAW, 0, k * src.shape[2], ("p (k n) -> p k n", {"k": k}), src,
                     n - RAW + 1 if n >= RAW else None)

            sp.dma_start(prow[0:124, 0, :], b_in.rearrange("l (c p) -> (l c) p", p=P)).then_inc(in_par, 16)
            for i in range(2):
                sp.dma_start(prow[0:124, 1 + i, :],
                             a_conv_w[i, :, :].rearrange("k (c p) -> (k c) p", p=P)).then_inc(in_par, 16)
            for at, src in ((G_MIX, norm_mix_g), (G_X, norm_x_g), (G_MEM, norm_mem_g), (G_FFN, norm_ffn_g),
                            (A_CB, a_conv_b), (A_LG, a_ln_g), (A_LB, a_ln_b)):
                m = src.shape[0] * src.shape[1] // P
                sp.dma_start(prow[at:at + m, 3, :], src.rearrange("l (c p) -> (l c) p", p=P)).then_inc(in_par, 16)
            sp.dma_start(prow[G_FIN:G_FIN + DB, 3, :], final_g.rearrange("(c p) -> c p", p=P)).then_inc(in_par, 16)
            sp.dma_start(prow[C_CW:C_CW + 24, 3, :],
                         c_conv_w.rearrange("l k (c p) -> (l k c) p", p=P)).then_inc(in_par, 16)
            sp.dma_start(xin, x[0].rearrange("(b p) d -> p b d", p=P)).then_inc(in_x, 16)
            sp.dma_start(min_, mem[0].rearrange("(b p) d -> p b d", p=P)).then_inc(in_mem, 16)

            sp.dma_start(router[:], moe_router[0].rearrange("(k p) e -> p k e", p=P)).then_inc(in_rt, 16)
            for lay in range(LAYERS):
                b = BASE[lay]
                if lay:
                    sp.wait_ge(h_lo_s, 6)
                sp.dma_start(vbias, b_in[lay:lay + 1, 2560:3328].to_broadcast([P, 768])).then_inc(in_vb, 16)
                for c in range(C_FFN):
                    n = b + c
                    if c < C_COUT:
                        dense(n, k8(w_in[lay], IN_BLOCKS[c]), 8)
                    elif c < C_GC:
                        dense(n, c_w_out[lay].rearrange("(k p) n -> p k n", p=P)[:, :, 512 * (c - C_COUT):512 * (c - C_COUT) + 512], 4)
                    elif c < C_AOUT:
                        dense(n, k8(w_in[lay], GC_BLOCK + c - C_GC), 8)
                    elif c < C_GA:
                        dense(n, a_w_out[lay].rearrange("(k p) n -> p k n", p=P)[:, :, 512 * (c - C_AOUT):512 * (c - C_AOUT) + 512], 4)
                    elif c < C_BOUT:
                        dense(n, k8(w_in[lay], GA_BLOCK + c - C_GA), 8)
                    elif c < C_GB:
                        dense(n, b_w_out[lay].rearrange("(k p) n -> p k n", p=P)[:, :, 512 * (c - C_BOUT):512 * (c - C_BOUT) + 512], 2)
                    elif c < C_WO:
                        dense(n, k8(w_in[lay], GB_BLOCK + c - C_GB), 8)
                    else:
                        w, at = [(w_o, C_WO), (xk_w, C_XK), (xq_w, C_XQ), (xv_w, C_XV), (xo_w, C_XO)][(c - C_WO) // 4]
                        dense(n, k8(w[lay], c - at), 8)
                if lay == 0:
                    f = b + C_FFN
                    w1v, w3v = (w[0].rearrange("(k p) n -> p k n", p=P) for w in (ffn_w1, ffn_w3))
                    w2v = ffn_w2[0].rearrange("(k p) n -> p k n", p=P)
                    dense(f, w1v[:, :, 0:256], 8)
                    dense(f + 1, w3v[:, :, 0:256], 8)
                    with sp.Fori(0, (FFB - 1) // 2) as i:
                        for c in range(6):
                            n0 = f + 2 + c
                            j = 1 + c // 3
                            if c % 3 < 2:
                                src = (w1v, w3v)[c % 3][:, :, bass.ds(512 * i + 256 * j, 256)]
                                k = 8
                            else:
                                src = w2v[:, bass.ds(4 * i + 2 * (j - 1), 2), :]
                                k = 2
                            load(n0 % RAW, 0, CW, ("p (k n) -> p k n", {"k": k}), src, 6 * i + n0 - RAW + 1)
                    dense(f + 3 * FFB - 1, w2v[:, 2 * FFB - 2:2 * FFB, :], 2)

            ew1, ew3 = (w[0].rearrange("e (k p) n -> e p k n", p=P) for w in (moe_w1, moe_w3))
            ew2 = moe_w2[0].rearrange("e (k p) n -> e p k n", p=P)

            def experts(r):
                first = MOE + NE * PER_E * r

                def up(w, e, f, half, c):
                    n0 = first + c
                    load(n0 % RAW, 0, CW, ("p (k n) -> p k n", {"k": 4}),
                         w[bass.ds(e, 1), :, 4 * half:4 * half + 4, 512 * f:512 * f + 512]
                         .rearrange("e p k n -> p (e k) n"), PER_E * e + n0 - RAW + 1)

                def down(e, f, half, c):
                    n0 = first + c
                    load(n0 % RAW, 0, CW, ("p (k n) -> p k n", {"k": 2}),
                         ew2[bass.ds(e, 1), :, 4 * f + 2 * half:4 * f + 2 * half + 2, :]
                         .rearrange("e p k n -> p (e k) n"), PER_E * e + n0 - RAW + 1)

                with sp.Fori(0, NE) as e:
                    c = 0
                    for f in range(FSTEPS + 1):
                        if f < FSTEPS:
                            for w in (ew1, ew3):
                                for half in range(2):
                                    up(w, e, f, half, c)
                                    c += 1
                        if f:
                            for half in range(2):
                                down(e, f - 1, half, c)
                                c += 1

            experts(0)
            sp.wait_ge(count_ready, 1)
            most = sp.value_load(cntu[0:1, 0:1])
            with sp.If(most > SLOTS):
                experts(1)
            with sp.Else():
                sp.nop()
            for b in range(TB):
                sp.wait_ge(fo_act if b else fo_ready, 2)
                sp.dma_start(out[0, b * P:(b + 1) * P, :], yout[:, b, :]).then_inc(out_sent, 16)
            sp.wait_ge(out_sent, 32)

        @block.gpsimd
        def _(gp):
            gp.memset(ident[:], 0.0).then_inc(const, 1)
            gp.memset(ones[:], 1.0 / D).then_inc(const, 1)
            gp.iota(dist, pattern=[[-1, S]], base=P, channel_multiplier=1).then_inc(const, 1)
            gp.wait_ge(const, 3)
            gp.affine_select(out=ident[:], in_=ident[:], compare_op=ALU.not_equal, fill=1.0, base=0,
                             pattern=[[-1, P]], channel_multiplier=1).then_inc(const, 1)

            for lay in range(LAYERS):
                b = BASE[lay]
                if lay:
                    gp.wait_ge(h_lo_s, 8)
                else:
                    gp.wait_ge(tr_done, 9)
                gp.memset(apad[:, :, 0:KA - 1], 0.0).then_inc(pads, 1)
                gp.memset(cpad[:, :, 0:KC - 1], 0.0).then_inc(pads, 1)
                done = 24 * lay
                for branch, at in enumerate((C_GC, C_GA, C_GB)):
                    for i in range(4):
                        s_, val = taken(b + at + i)
                        gp.wait_ge(s_, val)
                        yb, mb, gb = Y[:, 2 * i:2 * i + 2, :], merged[:, 2 * i:2 * i + 2, :], sg[:, i % 2, :, :]
                        if branch == 0:
                            gp.tensor_tensor(mb, gb, yb, ALU.mult).then_inc(gated, 2)
                            done += 2
                        else:
                            gp.tensor_tensor(yb, gb, yb, ALU.mult).then_inc(gated, 1)
                            done += 1
                            gp.wait_ge(gated, done)
                            gp.tensor_tensor(mb, mb, yb, ALU.add).then_inc(gated, 1)
                            done += 1

            gp.wait_ge(h_lo_s, 12)
            gp.iota(iota, pattern=[[1, P]], base=0, channel_multiplier=0,
                    allow_small_or_imprecise_dtypes=True).then_inc(rt_const, 1)
            gp.iota(iota8, pattern=[[1, NE]], base=0, channel_multiplier=0,
                    allow_small_or_imprecise_dtypes=True).then_inc(rt_const, 1)
            gp.memset(allone, 1.0).then_inc(rt_const, 1)
            gp.wait_ge(rt_const, 3)
            gp.affine_select(out=strict, in_=allone, compare_op=ALU.is_gt, fill=0.0, base=0,
                             pattern=[[1, P]], channel_multiplier=-1).then_inc(rt_const, 1)

        @block.scalar
        def _(act):
            def split_at(slot, n, raw_value, used, words=CW):
                act.wait_ge(w_raw[slot], raw_value)
                if used is not None:
                    act.wait_ge(w_used, used)
                act.activation(whi[:, n % SPLIT, 0:words], raw[:, slot, 0:words], ACT.Copy).then_inc(hi_ready, 1)

            def split(n):
                words = 1024 if local(n)[1] in (C_BOUT, C_BOUT + 1) else CW
                split_at(n % RAW, n, 16 * (n // RAW + 1), n - SPLIT + 1 if n >= SPLIT else None, words)

            def squares(q, pair):
                if q < 0:
                    act.wait_ge(mT_ready, pair + 1)
                    src = memhat
                else:
                    act.wait_ge(x_ready, 4 * q + pair + 1)
                    src = xT
                if q >= 0 and pair == 0:
                    act.wait_ge(ss_done, q + 1)
                act.activation(sq[:, 2 * pair:2 * pair + 2, :], src[:, 2 * pair:2 * pair + 2, :],
                               ACT.Square).then_inc(sq_ready, 1)

            def root(q):
                act.wait_ge(ms_ready, q + 2)
                act.activation(rstd[:], rstd[:], ACT.Sqrt).then_inc(rt_ready, 1)

            def norm_hi(q):
                for half in range(2):
                    act.wait_ge(hf_ready, 2 * q + half + 1)
                    act.activation(h_hl[:, 0, 4 * half:4 * half + 4, :], hf[:, 4 * half:4 * half + 4, :],
                                   ACT.Copy).then_inc(h_hi_s, 1)

            act.wait_ge(tr_done, 1)
            act.activation(par[:, 0:3, 0:124], bank[0][:, 0:384].rearrange("p (a b) -> p a b", a=3)[:, :, 0:124], ACT.Copy)
            act.activation(par[:, 3, 0:120], bank[0][:, 384:504], ACT.Copy).then_inc(par_ready, 1)
            for i in range(4):
                act.wait_ge(tr_done, 6 + i)
                act.activation(memhat[:, 2 * i:2 * i + 2, :], bank[5 + i if i < 3 else 0][:]
                               .rearrange("p (a b) -> p a b", a=2), ACT.Copy).then_inc(mT_ready, 1)
            for i in range(4):
                squares(-1, i)
            root(-1)
            for i in range(4):
                squares(0, i)
            for n in range(SPLIT):
                split(n)
            root(0)
            norm_hi(0)

            def bias(lay, cblock):
                return par[:, 0, 62 * lay + cblock:62 * lay + cblock + 1]

            def take(n, dst, func, lay, block_):
                src = bank[2 * (n % 2)]
                for i in range(2):
                    ins = act.activation(dst[i], src[:, 256 * i:256 * i + 256], func,
                                         bias=bias(lay, 2 * block_ + i))
                ins.then_inc(out_act, 1)

            def head_exp(lay, h):
                k = 4 * lay + h
                act.wait_ge(mx_ready, k + 1)
                if k:
                    act.wait_ge(o_ready, k)
                act.activation(prob0, prob0, ACT.Exp, bias=small[:, 0:1], accum_out=small[:, 4:5])
                act.activation(prob1, prob1, ACT.Exp, bias=small[:, 1:2], accum_out=small[:, 5:6])\
                   .then_inc(pr_ready, 1)

            def head_pT(lay, h):
                act.wait_ge(pt_done, 4 * lay + h + 1)
                act.activation(pT0, bank[4][:, 0:384].rearrange("p (a b) -> p a b", a=3), ACT.Copy)
                act.activation(pT1[:, 0:2, :], bank[5][:].rearrange("p (a b) -> p a b", a=2), ACT.Copy)
                act.activation(pT1[:, 2, :], bank[6][:, 0:256], ACT.Copy).then_inc(pT_ready, 1)

            def post(n):
                lay, c = local(n)
                b = BASE[lay]
                if c in (0, 2):
                    act.wait_ge(w_used, n + 1)
                    take(n, [agate[:, c + i, :] for i in range(2)], ACT.Sigmoid, lay, IN_BLOCKS[c])
                elif c in (4, 5):
                    act.wait_ge(w_used, n + 1)
                    take(n, [cb[:, 2 * (c - 4) + i, :] for i in range(2)], ACT.Identity, lay, IN_BLOCKS[c])
                elif c in (6, 8):
                    act.wait_ge(w_used, n + 1)
                    take(n, [ccv[:, c - 6 + i, :] for i in range(2)], ACT.Identity, lay, IN_BLOCKS[c])
                elif C_QKV <= c < C_QKV + 6:
                    act.wait_ge(w_used, n + 1)
                    dst = qT if c < C_QKV + 3 else kT
                    at = 2 * ((c - C_QKV) % 3)
                    take(n, [dst[:, at + i, :] for i in range(2)], ACT.Identity, lay, IN_BLOCKS[c])
                elif c in (C_COUT, C_COUT + 1, C_AOUT, C_AOUT + 1, C_BOUT, C_BOUT + 1):
                    i = c - [a for a in (C_COUT, C_AOUT, C_BOUT) if c in (a, a + 1)][0]
                    act.wait_ge(w_used, n + 1)
                    if c >= C_AOUT:
                        act.wait_ge(gated, 24 * lay + (8 if c < C_BOUT else 16))
                    for k in range(2):
                        ins = act.activation(Y[:, 4 * i + 2 * k:4 * i + 2 * k + 2, :],
                                             bank[2 * (n % 2) + k][:].rearrange("p (a b) -> p a b", a=2), ACT.Copy)
                    ins.then_inc(out_act, 1)
                elif c in range(C_GC, C_AOUT) or c in range(C_GA, C_BOUT) or c in range(C_GB, C_WO):
                    branch = 0 if c < C_AOUT else 1 if c < C_BOUT else 2
                    i = c - (C_GC, C_GA, C_GB)[branch]
                    done = 4 * branch + i
                    act.wait_ge(w_used, n + 1)
                    if done < 2:
                        act.wait_ge(conv_a, KA * AB * (lay + 1))
                    else:
                        act.wait_ge(gated, 24 * lay + 2 * (done - 1))
                    take(n, [sg[:, i % 2, k, :] for k in range(2)], ACT.Sigmoid, lay,
                         (GC_BLOCK, GA_BLOCK, GB_BLOCK)[branch] + i)
                elif C_XK <= c < C_XV + 4:
                    act.wait_ge(w_used, n + 1)
                    src = bank[2 * (n % 2)][:].rearrange("p (a b) -> p a b", a=2)
                    if c < C_XQ:
                        dst = kx[:, 2 * (c - C_XK):2 * (c - C_XK) + 2, :]
                    elif c < C_XV:
                        dst = qx[:, 2 * (c - C_XQ):2 * (c - C_XQ) + 2, :]
                    else:
                        dst = vx[:, :, 256 * (c - C_XV):256 * (c - C_XV) + 256]
                    act.activation(dst, src, ACT.Copy).then_inc(out_act, 1)
                if c == C_QKV:
                    act.wait_ge(c_f, lay + 1)
                    act.activation(c_hi, cacc, ACT.Copy).then_inc(c_hi_s, 1)
                if c == C_COUT + 1:
                    act.wait_ge(ln_xc, lay + 1)
                    act.activation(asq, aacc, ACT.Square).then_inc(ln_sq, 1)
                if c == C_GC + 1:
                    act.wait_ge(ln_var, lay + 1)
                    act.activation(rstd[:], rstd[:], ACT.Sqrt).then_inc(ln_rt, 1)
                    act.wait_ge(ln_y, lay + 1)
                    for k in range(AB):
                        ins = act.activation(asq[:, k, :], aacc[:, k, :], ACT.Silu,
                                             scale=par[:, 3, A_LG + 4 * lay + k:A_LG + 4 * lay + k + 1],
                                             bias=par[:, 3, A_LB + 4 * lay + k:A_LB + 4 * lay + k + 1])
                    ins.then_inc(a_f, 1)
                    act.wait_ge(a_f, lay + 1)
                    act.activation(a_hi, asq, ACT.Copy).then_inc(a_hi_s, 1)
                for h in range(HEADS):
                    if c == HEAD_AT[h]:
                        head_exp(lay, h)
                    if c == HEAD_AT[h] + 2:
                        head_pT(lay, h)
                if c == OT_AT:
                    act.wait_ge(oT_done, lay + 1)
                    act.activation(o_hi, bank[4][:].rearrange("p (a b) -> p a b", a=2), ACT.Copy).then_inc(o_hi_s, 1)
                if c == C_WO - 1:
                    for half in range(2):
                        act.wait_ge(gated, 24 * lay + 20 + 4 * half)
                        act.activation(h_hl[:, 0, 4 * half:4 * half + 4, :], merged[:, 4 * half:4 * half + 4, :],
                                       ACT.Copy).then_inc(mg_hi_s, 1)
                if C_WO <= c < C_XK:
                    squares(3 * lay + 1, c - C_WO)
                if c == C_WO + 1:
                    for half in range(2):
                        act.wait_ge(mf_ready, 2 * lay + half + 1)
                        act.activation(m_hi[:, 4 * half:4 * half + 4, :], hf[:, 4 * half:4 * half + 4, :],
                                       ACT.Copy).then_inc(m_hi_s, 1)
                if c == C_XK:
                    root(3 * lay + 1)
                    norm_hi(3 * lay + 1)
                if c == C_XV:
                    for i in range(XH * TB):
                        act.wait_ge(xm_ready, 8 * lay + i + 1)
                        act.activation(probx[:, i, :], bank[4 + i // 2][:, 256 * (i % 2):256 * (i % 2) + 256],
                                       ACT.Exp, scale=1.0 / 16, bias=small[:, 8 + i:9 + i],
                                       accum_out=small[:, 16 + i:17 + i]).then_inc(xp_ready, 1)
                if c == C_XV + 2:
                    for i in range(4):
                        act.wait_ge(xpt_done, 4 * lay + i + 1)
                        act.activation(pTx[:, 2 * i:2 * i + 2, :], bank[4 + i][:].rearrange("p (a b) -> p a b", a=2),
                                       ACT.Copy).then_inc(xpT_ready, 1)
                if c == C_XV + 3:
                    for i in range(4):
                        act.wait_ge(xpv_done, 4 * lay + i + 1)
                        act.activation(h_hl[:, 0, 2 * i:2 * i + 2, :], bank[4 + i][:].rearrange("p (a b) -> p a b", a=2),
                                       ACT.Copy).then_inc(xo_hi_s, 1)
                if C_XO <= c < C_FFN:
                    squares(3 * lay + 2, c - C_XO)
                if c == C_FFN - 1:
                    root(3 * lay + 2)
                    norm_hi(3 * lay + 2)

            def ffn_act(i, j, f0):
                act.wait_ge(w_used, f0)
                act.activation(sil[:, j, :], bank[2 * j][:], ACT.Silu).then_inc(silu_s, 1)
                act.wait_ge(g_s, i + 1)
                act.activation(g_hi[:, j, :], gf[:, j, :], ACT.Copy).then_inc(g_hi_s, 1)

            for lay in range(LAYERS):
                b = BASE[lay]
                for n in range(b + SPLIT, b + C_FFN):
                    post(n - SPLIT)
                    split(n)
                if lay == 0:
                    f = b + C_FFN
                    for k in range(3):
                        post(f - 3 + k)
                        if k < 2:
                            split(f + k)
                    with act.Fori(0, (FFB - 1) // 2) as i:
                        for c in range(6):
                            n0 = f + 2 + c
                            if c == 2:
                                ffn_act(2 * i, 0, 6 * i + f + 2)
                            if c == 4:
                                ffn_act(2 * i + 1, 1, 6 * i + n0 - 2)
                            split_at(n0 % RAW, n0, 16 * i + 16 * (n0 // RAW + 1), 6 * i + n0 - SPLIT + 1)
                    split(f + 3 * FFB - 1)
                    ffn_act(FFB - 1, 0, f + 3 * FFB - 2)
                    split(BASE[1])
                    split(BASE[1] + 1)
                    for i in range(4):
                        squares(3, i)
                    root(3)
                    norm_hi(3)
                    split(BASE[1] + 2)
                else:
                    for n in range(MOE - 3, MOE):
                        post(n)

            for i in range(4):
                act.wait_ge(ht_done, i + 1)
                act.activation(htok[:, i // 2, 512 * (i % 2):512 * (i % 2) + 512], bank[i][:], ACT.Copy)\
                   .then_inc(ht_ready, 1)
            act.wait_ge(rl_ready, 1)
            act.activation(wts[:, 2:4], wts[:, 0:2], ACT.Exp).then_inc(re_ready, 1)

            def experts(r):
                first = MOE + NE * PER_E * r
                for i in range(4):
                    act.wait_ge(wt_done, 4 * r + i + 1)
                    act.activation(wselT[:, 1 + 2 * i:3 + 2 * i, :], bank[i][:].rearrange("p (a b) -> p a b", a=2),
                                   ACT.Copy).then_inc(wt_ready, 1)

                def gathered(count):
                    act.wait_ge(ga_done, count)
                    for k in range(2):
                        ins = act.activation(he_hi[:, 512 * k:512 * k + 512], bank[2 + k][:], ACT.Copy)
                    ins.then_inc(he_hi_s, 1)

                def transposed(count):
                    act.wait_ge(e_tr, count)
                    act.activation(eT_hi, bank[6][:], ACT.Copy).then_inc(e_hi, 1)

                gathered(9 * r + 1)
                with act.Fori(0, NE) as e:
                    n_e = PER_E * e + first
                    k_e = FSTEPS * e + NE * FSTEPS * r
                    for c in range(PER_E):
                        if c == 2:
                            act.wait_ge(w_used, n_e)
                            act.wait_ge(y_zero, r + 1)
                            act.wait_ge(y_add, 4 * e + 36 * r + 1)
                            for k in range(2):
                                ins = act.activation(y[:, 512 * k:512 * k + 512], bank[4 + k][:], ACT.Copy)
                            ins.then_inc(y_ev, 1)
                        for f in range(FSTEPS):
                            w1b = 1 if f == 0 else 6 * f - 1
                            if c == w1b + SPLIT:
                                act.wait_ge(w_used, n_e + w1b + 1)
                                if f > 1:
                                    act.wait_ge(e_g, k_e + f - 1)
                                act.activation(esil[:, f % 2, :], bank[2 * (f % 2)][:], ACT.Silu).then_inc(e_silu, 1)
                            if f and c == w1b + SPLIT:
                                transposed(k_e + f)
                        n0 = first + c
                        split_at(n0 % RAW, n0, 7 * 16 * e + 16 * (n0 // RAW + 1), n_e + c - SPLIT + 1)
                    transposed(k_e + FSTEPS)
                    gathered(e + 9 * r + 2)
                act.wait_ge(w_used, first + NE * PER_E)
                act.wait_ge(y_add, 4 * NE + 36 * r + 1)
                for k in range(2):
                    ins = act.activation(y[:, 512 * k:512 * k + 512], bank[4 + k][:], ACT.Copy)
                ins.then_inc(y_ev, 1)
                act.wait_ge(y_add, 36 * (r + 1) + 1)

            experts(0)
            act.wait_ge(count_ready, 1)
            most = act.value_load(cntu[0:1, 0:1])
            with act.If(most > SLOTS):
                experts(1)
            with act.Else():
                act.nop()

            for i in range(4):
                if i == 0:
                    act.wait_ge(ss_done, 7)
                act.activation(sq[:, 2 * i:2 * i + 2, :], xT[:, 2 * i:2 * i + 2, :], ACT.Square).then_inc(sq_ready, 1)
            root(6)
            for i in range(2):
                act.wait_ge(fo_done, 3 + i)
                act.activation(yout[:, 1, 512 * i:512 * i + 512], bank[2 + i][:], ACT.Copy).then_inc(fo_act, 1)

        @block.vector
        def _(dve):
            own = [0]

            def mine(ins):
                own[0] += 1
                ins.then_inc(dve_own, 1)

            def settled():
                dve.wait_ge(dve_own, own[0])

            def split_at(slot, n, value, words=CW):
                dve.wait_ge(hi_ready, value)
                dve.tensor_tensor(wlo[:, n % SPLIT, 0:words], raw[:, slot, 0:words],
                                  whi[:, n % SPLIT, 0:words].bitcast(F32), ALU.subtract).then_inc(lo_ready, 1)

            def split(n):
                split_at(n % RAW, n, n + 1, 1024 if local(n)[1] in (C_BOUT, C_BOUT + 1) else CW)

            def mean_sq(q):
                dve.wait_ge(ss_done, q + 2)
                dve.tensor_scalar(rstd[:], bank[7][:, 0:256], EPS, None, ALU.add).then_inc(ms_ready, 1)
                dve.wait_ge(rt_ready, q + 2)
                mine(dve.reciprocal(rstd[:], rstd[:]))
                settled()

            def norm(q, gain):
                mean_sq(q)
                for half in range(2):
                    for c in range(4 * half, 4 * half + 4):
                        ins = dve.scalar_tensor_tensor(hf[:, c, :], xT[:, c, :], par[:, 3, gain + c:gain + c + 1],
                                                       rstd[:], op0=ALU.mult, op1=ALU.mult)
                    ins.then_inc(hf_ready, 1)

            def norm_lo(q):
                for half in range(2):
                    dve.wait_ge(h_hi_s, 2 * q + half + 1)
                    dve.tensor_tensor(h_hl[:, 1, 4 * half:4 * half + 4, :], hf[:, 4 * half:4 * half + 4, :],
                                      h_hl[:, 0, 4 * half:4 * half + 4, :].bitcast(F32), ALU.subtract)\
                       .then_inc(h_lo_s, 1)

            dve.wait_ge(const, 4)
            mine(dve.tensor_scalar(ban[:, 0, :], dist, 0.0, NEG, ALU.is_lt, ALU.mult))
            mine(dve.tensor_scalar(ban[:, 1, :], dist, float(P), NEG, ALU.is_gt, ALU.mult))
            settled()
            mine(dve.tensor_tensor(mask[:, 0, :], ban[:, 0, :], ban[:, 1, :], ALU.add))
            for g, dilation in ((1, 4), (2, 16)):
                mine(dve.tensor_scalar(rest, dist, dilation - 1, None, ALU.bitwise_and))
                settled()
                mine(dve.tensor_scalar(ban[:, 1, :], rest, 0.0, NEG, ALU.is_gt, ALU.mult))
                settled()
                mine(dve.tensor_tensor(mask[:, g, :], ban[:, 0, :], ban[:, 1, :], ALU.add))
                settled()
            for i in range(4):
                dve.wait_ge(tr_done, 2 + i)
                dve.tensor_copy(xT[:, 2 * i:2 * i + 2, :], bank[1 + i][:].rearrange("p (a b) -> p a b", a=2))\
                   .then_inc(x_ready, 1)
            mean_sq(-1)
            mine(dve.tensor_tensor(memhat[:], memhat[:], rstd[:].unsqueeze(1).to_broadcast([P, DB, S]), ALU.mult))
            settled()
            for n in range(SPLIT):
                split(n)
            dve.wait_ge(par_ready, 1)
            norm(0, G_MIX)
            norm_lo(0)

            def residual(n, lay, pair):
                dve.wait_ge(w_used, n + 1)
                xb = xT[:, 2 * pair:2 * pair + 2, :]
                dve.tensor_tensor(xb, bank[2 * (n % 2)][:].rearrange("p (a b) -> p a b", a=2), xb, ALU.add)\
                   .then_inc(x_ready, 1)

            taps = [0, 0]

            def tap_a(lay, k):
                for c in range(AB):
                    w = par[:, 1 + lay, 4 * k + c:4 * k + c + 1]
                    src = apad[:, c, k:k + S]
                    if k == 0:
                        ins = dve.tensor_scalar(aacc[:, c, :], src, w, par[:, 3, A_CB + 4 * lay + c:A_CB + 4 * lay + c + 1],
                                                ALU.mult, ALU.add)
                    else:
                        dve.wait_ge(conv_a, taps[0] - AB + 1)
                        ins = dve.scalar_tensor_tensor(aacc[:, c, :], src, w, aacc[:, c, :], op0=ALU.mult, op1=ALU.add)
                    ins.then_inc(conv_a, 1)
                    taps[0] += 1

            def tap_c(lay, k):
                for c in range(AB):
                    at = C_CW + 12 * lay + 4 * k + c
                    w = par[:, 3, at:at + 1]
                    src = cpad[:, c, k:k + S]
                    if k == 0:
                        ins = dve.tensor_scalar(cacc[:, c, :], src, w, None, ALU.mult)
                    else:
                        dve.wait_ge(conv_c, taps[1] - AB + 1)
                        ins = dve.scalar_tensor_tensor(cacc[:, c, :], src, w, cacc[:, c, :], op0=ALU.mult, op1=ALU.add)
                    ins.then_inc(conv_c, 1)
                    taps[1] += 1

            def head_mask(lay, h):
                k = 4 * lay + h
                dve.wait_ge(sc_done, k + 1)
                mine(dve.scalar_tensor_tensor(prob0, bank[4][:, 0:384].rearrange("p (a b) -> p a b", a=3), 0.125,
                                              mask[:, :, P:S], op0=ALU.mult, op1=ALU.add))
                mine(dve.scalar_tensor_tensor(prob1[:, 0:2, :], bank[5][:].rearrange("p (a b) -> p a b", a=2), 0.125,
                                              mask[:, 0:2, :], op0=ALU.mult, op1=ALU.add))
                mine(dve.scalar_tensor_tensor(prob1[:, 2, :], bank[6][:, 0:256], 0.125, mask[:, 2, :],
                                              op0=ALU.mult, op1=ALU.add))
                settled()
                mine(dve.tensor_reduce(small[:, 2:3], prob0.rearrange("p a b -> p (a b)"), AX.X, ALU.max))
                mine(dve.tensor_reduce(small[:, 3:4], prob1.rearrange("p a b -> p (a b)"), AX.X, ALU.max))
                settled()
                dve.tensor_scalar(small[:, 0:2], small[:, 2:4], -1.0, None, ALU.mult).then_inc(mx_ready, 1)

            def head_out(lay, h):
                k = 4 * lay + h
                dve.wait_ge(pv_done, k + 1)
                mine(dve.reciprocal(small[:, 6:8], small[:, 4:6]))
                settled()
                dve.tensor_scalar(otok[:, 0, DH * h:DH * h + DH], bank[7][:, 0:64], small[:, 6:7], None, ALU.mult)
                dve.tensor_scalar(otok[:, 1, DH * h:DH * h + DH], bank[7][:, 64:128], small[:, 7:8], None, ALU.mult)\
                   .then_inc(o_ready, 1)

            def post(n):
                lay, c = local(n)
                b = BASE[lay]
                src = bank[2 * (n % 2)]
                bcol = lambda block_, i: par[:, 0, 62 * lay + 2 * block_ + i:62 * lay + 2 * block_ + i + 1]
                if c in (1, 3, 7, 9):
                    dve.wait_ge(w_used, n + 1)
                    s_, val = taken(n - 1)
                    dve.wait_ge(s_, val)
                    dve.wait_ge(pads, 2 * (lay + 1))
                    for i in range(2):
                        at = (c - 1 if c < 4 else c - 7) + i
                        dst = (apad[:, at, KA - 1:] if c < 4 else cpad[:, at, KC - 1:])
                        gate = (agate if c < 4 else ccv)[:, at, :]
                        ins = dve.scalar_tensor_tensor(dst, src[:, 256 * i:256 * i + 256], bcol(IN_BLOCKS[c], i), gate,
                                                       op0=ALU.add, op1=ALU.mult)
                    ins.then_inc(out_dve, 1)
                elif c in (16, 17, 18):
                    dve.wait_ge(w_used, n + 1)
                    dve.wait_ge(in_vb, 16 * (lay + 1))
                    g = c - 16
                    dve.tensor_tensor(vtok[:, :, 256 * g:256 * g + 256], src[:].rearrange("p (a b) -> p a b", a=2),
                                      vbias[:, 256 * g:256 * g + 256].unsqueeze(1).to_broadcast([P, TB, 256]), ALU.add)\
                       .then_inc(out_dve, 1)
                elif C_WO <= c < C_XK:
                    residual(n, lay, c - C_WO)
                elif C_XO <= c < C_FFN:
                    residual(n, lay, c - C_XO)
                if c == 3:
                    s_, val = taken(n)
                    dve.wait_ge(s_, val)
                if c == 9:
                    s_, val = taken(n)
                    dve.wait_ge(s_, val)
                    for k in range(KC):
                        tap_c(lay, k)
                    dve.wait_ge(conv_c, taps[1])
                    s_, val = taken(b + 5)
                    dve.wait_ge(s_, val)
                    dve.tensor_tensor(cacc, cacc, cb, ALU.mult).then_inc(c_f, 1)
                if 3 <= c < 3 + (KA + 1) // 2:
                    for k in range(2 * (c - 3), min(KA, 2 * (c - 3) + 2)):
                        tap_a(lay, k)
                if c == C_QKV:
                    dve.wait_ge(c_hi_s, lay + 1)
                    dve.tensor_tensor(c_lo, cacc, c_hi.bitcast(F32), ALU.subtract).then_inc(c_lo_s, 1)
                if c == C_COUT + 1:
                    dve.wait_ge(ln_st, 2 * lay + 1)
                    dve.scalar_tensor_tensor(aacc, bank[ln_bank(b + 21)][:, 0:256].unsqueeze(1).to_broadcast([P, AB, S]), -float(D) / AW,
                                             aacc, op0=ALU.mult, op1=ALU.add).then_inc(ln_xc, 1)
                if c == C_GC + 1:
                    dve.wait_ge(ln_st, 2 * lay + 2)
                    dve.tensor_scalar(rstd[:], bank[ln_bank(b + 21)][:, 0:256], float(D) / AW, EPS, ALU.mult, ALU.add)\
                       .then_inc(ln_var, 1)
                    dve.wait_ge(ln_rt, lay + 1)
                    mine(dve.reciprocal(rstd[:], rstd[:]))
                    settled()
                    dve.tensor_tensor(aacc, aacc, rstd[:].unsqueeze(1).to_broadcast([P, AB, S]), ALU.mult).then_inc(ln_y, 1)
                    dve.wait_ge(a_hi_s, lay + 1)
                    dve.tensor_tensor(a_lo, asq, a_hi.bitcast(F32), ALU.subtract).then_inc(a_lo_s, 1)
                for h in range(HEADS):
                    if c == HEAD_AT[h] + 3:
                        head_out(lay, h)
                for h in range(HEADS):
                    if c == HEAD_AT[h]:
                        head_mask(lay, h)
                if c == OT_AT:
                    dve.wait_ge(o_hi_s, lay + 1)
                    dve.tensor_tensor(o_lo, bank[4][:].rearrange("p (a b) -> p a b", a=2), o_hi.bitcast(F32),
                                      ALU.subtract).then_inc(o_lo_s, 1)
                if c == C_WO - 1:
                    for half in range(2):
                        dve.wait_ge(mg_hi_s, 2 * lay + half + 1)
                        dve.tensor_tensor(h_hl[:, 1, 4 * half:4 * half + 4, :], merged[:, 4 * half:4 * half + 4, :],
                                          h_hl[:, 0, 4 * half:4 * half + 4, :].bitcast(F32), ALU.subtract)\
                           .then_inc(mg_lo_s, 1)
                if c == C_WO:
                    for half in range(2):
                        for k in range(4 * half, 4 * half + 4):
                            at = G_MEM + 8 * lay + k
                            ins = dve.tensor_scalar(hf[:, k, :], memhat[:, k, :], par[:, 3, at:at + 1], None, ALU.mult)
                        ins.then_inc(mf_ready, 1)
                if c == C_WO + 1:
                    for half in range(2):
                        dve.wait_ge(m_hi_s, 2 * lay + half + 1)
                        dve.tensor_tensor(m_lo[:, 4 * half:4 * half + 4, :], hf[:, 4 * half:4 * half + 4, :],
                                          m_hi[:, 4 * half:4 * half + 4, :].bitcast(F32), ALU.subtract).then_inc(m_lo_s, 1)
                if c == C_XK:
                    dve.wait_ge(m_lo_s, 2 * lay + 2)
                    norm(3 * lay + 1, G_X + 8 * lay)
                    norm_lo(3 * lay + 1)
                if c == C_XV:
                    for i in range(4):
                        dve.wait_ge(xs_done, 4 * lay + i + 1)
                        mine(dve.tensor_reduce(small[:, 24 + 2 * i:26 + 2 * i],
                                               bank[4 + i][:].rearrange("p (a b) -> p a b", a=2), AX.X, ALU.max))
                        settled()
                        dve.tensor_scalar(small[:, 8 + 2 * i:10 + 2 * i], small[:, 24 + 2 * i:26 + 2 * i], -1.0 / 16, None,
                                          ALU.mult).then_inc(xm_ready, 2)
                    for i in range(4):
                        dve.wait_ge(xp_ready, 8 * lay + 2 * i + 2)
                        mine(dve.reciprocal(small[:, 16 + 2 * i:18 + 2 * i], small[:, 16 + 2 * i:18 + 2 * i]))
                        settled()
                        for k in range(2):
                            ins = dve.tensor_scalar(probx[:, 2 * i + k, :], probx[:, 2 * i + k, :],
                                                    small[:, 16 + 2 * i + k:17 + 2 * i + k], None, ALU.mult)
                        ins.then_inc(xn_ready, 1)
                if c == C_XV + 3:
                    for i in range(4):
                        dve.wait_ge(xo_hi_s, 4 * lay + i + 1)
                        dve.tensor_tensor(h_hl[:, 1, 2 * i:2 * i + 2, :], bank[4 + i][:].rearrange("p (a b) -> p a b", a=2),
                                          h_hl[:, 0, 2 * i:2 * i + 2, :].bitcast(F32), ALU.subtract).then_inc(xo_lo_s, 1)
                if c == C_FFN - 1:
                    if lay == 0:
                        dve.memset(zerosf, 0.0).then_inc(z_ready, 1)
                    norm(3 * lay + 2, G_FFN + 8 * lay)
                    norm_lo(3 * lay + 2)

            def ffn_dve(i, j):
                dve.wait_ge(silu_s, i + 1)
                dve.tensor_tensor(gf[:, j, :], bank[2 * j + 1][:], sil[:, j, :], ALU.mult).then_inc(g_s, 1)
                dve.wait_ge(g_hi_s, i + 1)
                dve.tensor_tensor(g_lo[:, j, :], gf[:, j, :], g_hi[:, j, :].bitcast(F32), ALU.subtract).then_inc(g_lo_s, 1)

            for lay in range(LAYERS):
                b = BASE[lay]
                for n in range(b + SPLIT, b + C_FFN):
                    post(n - SPLIT)
                    split(n)
                if lay == 0:
                    f = b + C_FFN
                    for k in range(3):
                        post(f - 3 + k)
                        if k < 2:
                            split(f + k)
                    with dve.Fori(0, (FFB - 1) // 2) as i:
                        for c in range(6):
                            n0 = f + 2 + c
                            if c == 2:
                                ffn_dve(2 * i, 0)
                            if c == 4:
                                ffn_dve(2 * i + 1, 1)
                            split_at(n0 % RAW, n0, 6 * i + n0 + 1)
                    split(f + 3 * FFB - 1)
                    ffn_dve(FFB - 1, 0)
                    split(BASE[1])
                    split(BASE[1] + 1)
                    for i in range(4):
                        dve.wait_ge(w_used, BASE[1])
                        xb = xT[:, 2 * i:2 * i + 2, :]
                        dve.tensor_tensor(xb, bank[4 + i][:].rearrange("p (a b) -> p a b", a=2), xb, ALU.add)\
                           .then_inc(x_ready, 1)
                    norm(3, G_MIX + 8)
                    norm_lo(3)
                    split(BASE[1] + 2)
                else:
                    for n in range(MOE - 3, MOE):
                        post(n)

            dve.wait_ge(rl_done, 1)
            mine(dve.tensor_copy(lg, bank[7][:, 256:272].rearrange("p (b e) -> p b e", e=NE)))
            settled()
            for b in range(TB):
                mine(dve.max(top[:, b, :], lg[:, b, :]))
            settled()
            for b in range(TB):
                mine(dve.max_index(idxu[:, b, :], top[:, b, :], lg[:, b, :]))
                mine(dve.tensor_tensor(wts[:, b:b + 1], top[:, b, 1:2], top[:, b, 0:1], ALU.subtract))
            settled()
            dve.tensor_copy(idxf, idxu[:]).then_inc(rl_ready, 1)
            dve.wait_ge(rl_ready, 1)
            dve.wait_ge(rt_const, 4)
            for b in range(TB):
                mine(dve.tensor_scalar(oh0[:, b, :], iota8, idxf[:, b, 0:1], None, ALU.is_equal))
                mine(dve.tensor_scalar(oh1[:, b, :], iota8, idxf[:, b, 1:2], None, ALU.is_equal))
            settled()
            dve.tensor_tensor(msk, oh0, oh1, ALU.add).then_inc(mk_ready, 1)
            dve.wait_ge(re_ready, 1)
            mine(dve.tensor_scalar(wts[:, 4:6], wts[:, 2:4], 1.0, None, ALU.add))
            settled()
            mine(dve.reciprocal(wts[:, 6:8], wts[:, 4:6]))
            settled()
            mine(dve.tensor_tensor(wts[:, 8:10], wts[:, 2:4], wts[:, 6:8], ALU.mult))
            for b in range(TB):
                mine(dve.tensor_scalar(comb[:, b, :], oh0[:, b, :], wts[:, 6 + b:7 + b], None, ALU.mult))
            settled()
            for b in range(TB):
                mine(dve.scalar_tensor_tensor(comb[:, b, :], oh1[:, b, :], wts[:, 8 + b:9 + b], comb[:, b, :],
                                              op0=ALU.mult, op1=ALU.add))
            dve.wait_ge(cnt_done, 1)
            mine(dve.tensor_scalar(posm, bank[7][:, 288:304].rearrange("p (b e) -> p b e", e=NE), 1.0, None, ALU.add))
            mine(dve.tensor_reduce(cntf, bank[7][:, 304:312], AX.X, ALU.max))
            dve.wait_ge(mk_ready, 1)
            settled()
            mine(dve.tensor_tensor(posm, posm, msk, ALU.mult))
            dve.tensor_copy(cntu[:], cntf).then_inc(count_ready, 1)

            def experts(r):
                first = MOE + NE * PER_E * r
                dve.tensor_scalar(posr, posm, -1.0 - SLOTS * r, None, ALU.add).then_inc(round_own, 1)
                if r == 0:
                    dve.memset(y, 0.0).then_inc(y_add, 1)
                    dve.wait_ge(y_add, 1)
                else:
                    dve.memset(y, 0.0)
                dve.memset(wselT[:, 0, :], 0.0)
                dve.memset(sel[:, :, NE, :], 0.0).then_inc(round_own, 1)
                dve.wait_ge(round_own, 2 * (r + 1))
                for e in range(NE):
                    for b in range(TB):
                        dve.tensor_scalar(sel[:, b, e, :], iota, posr[:, b, e:e + 1], None, ALU.is_equal)
                        ins = dve.tensor_scalar(wsel[:, b, e, :], iota, posr[:, b, e:e + 1], comb[:, b, e:e + 1],
                                                ALU.is_equal, ALU.mult)
                ins.then_inc(sel_ready, 1)

                def gathered(count):
                    dve.wait_ge(he_hi_s, count)
                    for k in range(2):
                        ins = dve.tensor_tensor(he_lo[:, 512 * k:512 * k + 512], bank[2 + k][:],
                                                he_hi[:, 512 * k:512 * k + 512].bitcast(F32), ALU.subtract)
                    ins.then_inc(he_lo_s, 1)

                def transposed(count):
                    dve.wait_ge(e_hi, count)
                    dve.tensor_tensor(eT_lo, bank[6][:], eT_hi.bitcast(F32), ALU.subtract).then_inc(e_lo, 1)

                def scattered(count, q):
                    dve.wait_ge(y_sc, count)
                    xb = xT[:, 2 * q:2 * q + 2, :]
                    dve.tensor_tensor(xb, bank[7][:].rearrange("p (a b) -> p a b", a=2), xb, ALU.add).then_inc(y_add, 1)

                gathered(9 * r + 1)
                with dve.Fori(0, NE) as e:
                    k_e = FSTEPS * e + NE * FSTEPS * r
                    for c in range(PER_E):
                        for f in range(FSTEPS):
                            w1b = 1 if f == 0 else 6 * f - 1
                            w3b = w1b + 2
                            if f and c == w1b + SPLIT:
                                transposed(k_e + f)
                            if c == w3b + SPLIT:
                                dve.wait_ge(e_silu, k_e + f + 1)
                                dve.wait_ge(w_used, PER_E * e + first + w3b + 1)
                                dve.tensor_tensor(eg, bank[2 * (f % 2) + 1][:], esil[:, f % 2, :], ALU.mult).then_inc(e_g, 1)
                            if f < 4 and c == w3b + SPLIT + (0 if f else 1):
                                scattered(4 * e + 36 * r + f + 1, f)
                        n0 = first + c
                        split_at(n0 % RAW, n0, PER_E * e + n0 + 1)
                    transposed(k_e + FSTEPS)
                    gathered(e + 9 * r + 2)
                for q in range(4):
                    scattered(36 * r + 4 * NE + q + 1, q)
                dve.wait_ge(y_add, 36 * (r + 1) + 1)

            settled()
            experts(0)
            most = dve.value_load(cntu[0:1, 0:1])
            with dve.If(most > SLOTS):
                experts(1)
            with dve.Else():
                dve.nop()
            mean_sq(6)
            for half in range(2):
                for c in range(4 * half, 4 * half + 4):
                    ins = dve.scalar_tensor_tensor(hf[:, c, :], xT[:, c, :], par[:, 3, G_FIN + c:G_FIN + c + 1],
                                                   rstd[:], op0=ALU.mult, op1=ALU.mult)
                ins.then_inc(hf_ready, 1)
            for i in range(2):
                dve.wait_ge(fo_done, 1 + i)
                dve.tensor_copy(yout[:, 0, 512 * i:512 * i + 512], bank[i][:]).then_inc(fo_ready, 1)

        @block.tensor
        def _(pe):
            def three(o, st, mv, start, stop, **kw):
                pe.matmul(o, st[0], mv[0], start=start, stop=False, **kw)
                pe.matmul(o, st[0], mv[1], start=False, stop=False, **kw)
                return pe.matmul(o, st[1], mv[0], start=False, stop=stop, **kw)

            def wt(n, k, cols, at, width):
                return tuple(w[:, n % SPLIT, k * cols + at:k * cols + at + width] for w in (whi, wlo))

            def parts(hi, lo, k):
                return hi[:, k, :], lo[:, k, :]

            h_hi, h_lo = h_hl[:, 0, :, :], h_hl[:, 1, :, :]

            def free(n):
                lay, c = local(n)
                if c >= 2:
                    s_, val = taken(n - 2)
                    pe.wait_ge(s_, val)

            def chunk_in(n):
                pe.wait_ge(lo_ready, n + 1)
                free(n)
                for o in range(2):
                    for k in range(DB):
                        ins = three(bank[2 * (n % 2)][:, 256 * o:256 * o + 256], wt(n, k, 256, 128 * o, 128),
                                    parts(h_hi, h_lo, k), k == 0, k == DB - 1)
                ins.then_inc(w_used, 1)

            def chunk_tok(n, hi, lo):
                pe.wait_ge(lo_ready, n + 1)
                free(n)
                for t in range(TB):
                    for k in range(DB):
                        tok = tuple(a[:, k, P * t:P * t + P] for a in (hi, lo))
                        ins = three(bank[2 * (n % 2)][:, 256 * t:256 * t + 256], tok, wt(n, k, 256, 0, 256),
                                    k == 0, k == DB - 1)
                ins.then_inc(w_used, 1)

            def chunk_mem(n):
                pe.wait_ge(lo_ready, n + 1)
                free(n)
                for o in range(2):
                    for k in range(DB):
                        ins = three(bank[2 * (n % 2)][:, 256 * o:256 * o + 256], wt(n, k, 256, 128 * o, 128),
                                    parts(m_hi, m_lo, k), k == 0, k == DB - 1)
                ins.then_inc(w_used, 1)

            def chunk_out(n, hi, lo, kb):
                pe.wait_ge(lo_ready, n + 1)
                free(n)
                for o in range(4):
                    for k in range(kb):
                        ins = three(bank[2 * (n % 2) + o // 2][:, 256 * (o % 2):256 * (o % 2) + 256],
                                    wt(n, k, 512, 128 * o, 128), parts(hi, lo, k), k == 0, k == kb - 1)
                ins.then_inc(w_used, 1)

            def stat(src, nb, to=7):
                for k in range(nb):
                    ins = pe.matmul(bank[to][:, 0:256], ones[:], src[:, k, :], start=k == 0, stop=k == nb - 1)
                return ins

            def norm_stat(q):
                pe.wait_ge(sq_ready, 4 * (q + 2))
                stat(sq, DB).then_inc(ss_done, 1)

            pe.wait_ge(const, 4)
            pe.wait_ge(in_par, 12 * 16)
            for t in range(4):
                rows = 120 if t == 3 else 124
                ins = pe.transpose(bank[0][:, P * t:P * t + rows], prow[0:rows, t, :], ident[0:rows, 0:rows])
            ins.then_inc(tr_done, 1)
            for src, s_, banks in ((xin, in_x, (1, 2, 3, 4)), (min_, in_mem, (5, 6, 7, 0))):
                pe.wait_ge(s_, 16)
                for i in range(4):
                    if banks[i] == 0:
                        pe.wait_ge(par_ready, 1)
                    for k in range(4):
                        c, t = 2 * i + k // 2, k % 2
                        ins = pe.transpose(bank[banks[i]][:, P * k:P * k + P], src[:, t, P * c:P * c + P], ident[:])
                    ins.then_inc(tr_done, 1)
            pe.wait_ge(mT_ready, 4)
            norm_stat(-1)
            pe.wait_ge(ms_ready, 1)
            norm_stat(0)

            def scores(lay, h):
                if h == 0:
                    s_, val = taken(BASE[lay] + 15)
                    pe.wait_ge(s_, val)
                for g in range(GROUPS):
                    c, p0 = 2 * g + h // 2, 64 * (h % 2)
                    q_, k_ = qT[p0:p0 + 64, c, :], kT[p0:p0 + 64, c, :]
                    pe.matmul(bank[4][:, P * g:P * g + P], q_[:, 0:P], k_[:, 0:P], start=True, stop=True)
                    o = bank[5][:, 256 * g:256 * g + 256] if g < 2 else bank[6][:, 0:256]
                    ins = pe.matmul(o, q_[:, P:S], k_, start=True, stop=True)
                ins.then_inc(sc_done, 1)

            def values(lay, h):
                k = 4 * lay + h
                pe.wait_ge(pr_ready, k + 1)
                for g in range(GROUPS):
                    pe.transpose(bank[4][:, P * g:P * g + P], prob0[:, g, :], ident[:])
                    for t in range(TB):
                        o = bank[5][:, 256 * g + P * t:256 * g + P * t + P] if g < 2 else bank[6][:, P * t:P * t + P]
                        ins = pe.transpose(o, prob1[:, g, P * t:P * t + P], ident[:])
                ins.then_inc(pt_done, 1)

            def weigh(lay, h):
                k = 4 * lay + h
                pe.wait_ge(pT_ready, k + 1)
                if h == 0:
                    s_, val = taken(BASE[lay] + 18)
                    pe.wait_ge(s_, val)
                for g in range(GROUPS):
                    at = 256 * g + DH * h
                    pe.matmul(bank[7][:, 0:64], pT0[:, g, :], vtok[:, 0, at:at + DH], start=g == 0, stop=g == GROUPS - 1)
                for g in range(GROUPS):
                    at = 256 * g + DH * h
                    for t in range(TB):
                        ins = pe.matmul(bank[7][:, 64:128], pT1[:, g, P * t:P * t + P], vtok[:, t, at:at + DH],
                                        start=g == 0 and t == 0, stop=g == GROUPS - 1 and t == TB - 1)
                ins.then_inc(pv_done, 1)

            for lay in range(LAYERS):
                b = BASE[lay]
                pe.wait_ge(h_lo_s, 6 * lay + 2)
                for c in range(C_FFN):
                    n = b + c
                    if c == C_COUT:
                        pe.wait_ge(c_lo_s, lay + 1)
                    if c == C_COUT + 2:
                        pe.wait_ge(conv_a, KA * AB * (lay + 1))
                        s_, val = taken(n - 2)
                        pe.wait_ge(s_, val)
                        stat(aacc, AB, ln_bank(n)).then_inc(ln_st, 1)
                    if c == C_GC + 2:
                        pe.wait_ge(ln_sq, lay + 1)
                        stat(asq, AB, ln_bank(n)).then_inc(ln_st, 1)
                    if c == C_AOUT:
                        pe.wait_ge(a_lo_s, lay + 1)
                    for h in range(HEADS):
                        if c == HEAD_AT[h] + 3:
                            values(lay, h)
                        if c == HEAD_AT[h] + 4:
                            weigh(lay, h)
                    for h in range(HEADS):
                        if c == HEAD_AT[h] + 1:
                            scores(lay, h)
                    if c == OT_AT + 1:
                        pe.wait_ge(o_ready, 4 * lay + 4)
                        for i in range(2):
                            for t in range(TB):
                                ins = pe.transpose(bank[4][:, 256 * i + P * t:256 * i + P * t + P],
                                                   otok[:, t, P * i:P * i + P], ident[:])
                        ins.then_inc(oT_done, 1)
                    if c == C_BOUT:
                        pe.wait_ge(o_lo_s, lay + 1)
                    if c == C_WO:
                        pe.wait_ge(mg_lo_s, 2 * lay + 2)
                    if c == C_XK:
                        pe.wait_ge(m_lo_s, 2 * lay + 2)
                    if c == C_XK + 1:
                        norm_stat(3 * lay + 1)
                    if c == C_XQ:
                        pe.wait_ge(h_lo_s, 6 * lay + 4)
                    if c == C_XV + 1:
                        for cc in (C_XK + 3, C_XQ + 3):
                            s_, val = taken(b + cc)
                            pe.wait_ge(s_, val)
                        for hh in range(XH):
                            for t in range(TB):
                                for k in range(2):
                                    ins = pe.matmul(bank[4 + hh][:, 256 * t:256 * t + 256],
                                                    qx[:, 2 * hh + k, P * t:P * t + P], kx[:, 2 * hh + k, :],
                                                    start=k == 0, stop=k == 1)
                            ins.then_inc(xs_done, 1)
                    if c == C_XV + 3:
                        for hh in range(XH):
                            pe.wait_ge(xn_ready, 4 * lay + hh + 1)
                            for m in range(TB):
                                for t in range(TB):
                                    ins = pe.transpose(bank[4 + hh][:, 256 * m + P * t:256 * m + P * t + P],
                                                       probx[:, 2 * hh + t, P * m:P * m + P], ident[:])
                            ins.then_inc(xpt_done, 1)
                    if c == C_XO:
                        s_, val = taken(b + C_XV + 3)
                        pe.wait_ge(s_, val)
                        for hh in range(XH):
                            pe.wait_ge(xpT_ready, 4 * lay + hh + 1)
                            for o in range(2):
                                for m in range(TB):
                                    at = 256 * hh + P * o
                                    ins = pe.matmul(bank[4 + hh][:, 256 * o:256 * o + 256], vx[:, m, at:at + P],
                                                    pTx[:, 2 * hh + m, :], start=m == 0, stop=m == TB - 1)
                            ins.then_inc(xpv_done, 1)
                        pe.wait_ge(xo_lo_s, 4 * lay + 4)
                    if 16 <= c < C_COUT:
                        chunk_tok(n, h_hi, h_lo)
                    elif C_XV <= c < C_XO:
                        chunk_tok(n, m_hi, m_lo)
                    elif C_XK <= c < C_XQ:
                        chunk_mem(n)
                    elif C_COUT <= c < C_GC:
                        chunk_out(n, c_hi, c_lo, AB)
                    elif C_AOUT <= c < C_GA:
                        chunk_out(n, a_hi, a_lo, AB)
                    elif C_BOUT <= c < C_GB:
                        chunk_out(n, o_hi, o_lo, 2)
                    else:
                        chunk_in(n)
                norm_stat(3 * lay + 2)
                pe.wait_ge(h_lo_s, 6 * lay + 6)
                if lay == 0:
                    f = b + C_FFN

                    def up(n0, value, bk):
                        pe.wait_ge(lo_ready, value)
                        for o in range(2):
                            for k in range(DB):
                                ins = three(bank[bk][:, 256 * o:256 * o + 256], wt(n0, k, 256, 128 * o, 128),
                                            parts(h_hi, h_lo, k), k == 0, k == DB - 1)
                        ins.then_inc(w_used, 1)

                    def down(n0, value, steps, j):
                        pe.wait_ge(lo_ready, value)
                        pe.wait_ge(g_lo_s, steps)
                        for o in range(DB):
                            for k in range(2):
                                hid = tuple(a[:, j, 256 * k:256 * k + 256] for a in (g_hi, g_lo))
                                ins = three(bank[4 + o // 2][:, 256 * (o % 2):256 * (o % 2) + 256],
                                            wt(n0, k, D, P * o, P), hid, False, False,
                                            skip_group_check=True)
                        ins.then_inc(w_used, 1)

                    up(f, f + 1, 0)
                    up(f + 1, f + 2, 1)
                    pe.wait_ge(z_ready, 1)
                    for o in range(4):
                        pe.matmul(bank[4 + o][:], zeros[:, 0:P], zeros, start=True, stop=False, skip_group_check=True)
                    with pe.Fori(0, (FFB - 1) // 2) as i:
                        for j in (1, 2):
                            c = 3 * (j - 1)
                            bk = 2 * (j % 2)
                            up(f + 2 + c, 6 * i + f + 3 + c, bk)
                            up(f + 3 + c, 6 * i + f + 4 + c, bk + 1)
                            down(f + 4 + c, 6 * i + f + 5 + c, 2 * i + j, (j - 1) % 2)
                    down(f + 3 * FFB - 1, f + 3 * FFB, FFB, (FFB - 1) % 2)
                    norm_stat(3)

            for i in range(4):
                for k in range(4):
                    c = 4 * (i % 2) + k
                    ins = pe.transpose(bank[i][:, P * k:P * k + P], hf[:, c, P * (i // 2):P * (i // 2) + P], ident[:])
                ins.then_inc(ht_done, 1)
            pe.wait_ge(in_rt, 16)
            for t in range(TB):
                for k in range(DB):
                    ins = pe.matmul(bank[7][:, 256 + NE * t:256 + NE * t + NE], hf[:, k, P * t:P * t + P], router[:, k, :],
                                    start=k == 0, stop=k == DB - 1)
            ins.then_inc(rl_done, 1)
            pe.wait_ge(mk_ready, 1)
            pe.wait_ge(rt_const, 4)
            pe.matmul(bank[7][:, 288:296], strict, msk[:, 0, :], start=True, stop=True)
            pe.matmul(bank[7][:, 296:304], allone, msk[:, 0, :], start=True, stop=False)
            pe.matmul(bank[7][:, 296:304], strict, msk[:, 1, :], start=False, stop=True)
            pe.matmul(bank[7][:, 304:312], allone, msk[:, 0, :], start=True, stop=False)
            pe.matmul(bank[7][:, 304:312], allone, msk[:, 1, :], start=False, stop=True).then_inc(cnt_done, 1)

            def experts(r):
                first = MOE + NE * PER_E * r
                pe.wait_ge(sel_ready, r + 1)
                if r == 0:
                    pe.wait_ge(ht_ready, 4)
                for i in range(4):
                    for k in range(4):
                        e, t = 2 * i + k // 2, k % 2
                        ins = pe.transpose(bank[i][:, P * k:P * k + P], wsel[:, t, e, :], ident[:])
                    ins.then_inc(wt_done, 1)
                for k in range(2):
                    ins = pe.matmul(bank[4 + k][:], y0[:, 0:P], y0, start=True, stop=True)
                ins.then_inc(y_zero, 1)

                def gather(e):
                    for c in range(DB):
                        for t in range(TB):
                            ins = pe.matmul(bank[2 + c // 4][:, P * (c % 4):P * (c % 4) + P], htok[:, t, P * c:P * c + P],
                                            sel[:, t, bass.ds(e, 1), :].rearrange("p a b -> p (a b)"),
                                            start=t == 0, stop=t == TB - 1)
                    ins.then_inc(ga_done, 1)

                def up(c, e, o):
                    n0 = first + c
                    half = c % 2
                    pe.wait_ge(lo_ready, PER_E * e + n0 + 1)
                    for k in range(4):
                        tok = tuple(a[:, P * (4 * half + k):P * (4 * half + k) + P] for a in (he_hi, he_lo))
                        ins = three(o, tok, wt(n0, k, 512, 0, 512), half == 0 and k == 0, half == 1 and k == 3)
                    ins.then_inc(w_used, 1)

                def turn(f, k_e):
                    pe.wait_ge(e_g, k_e + f + 1)
                    for k in range(4):
                        ins = pe.transpose(bank[6][:, P * k:P * k + P], eg[:, P * k:P * k + P], ident[:])
                    ins.then_inc(e_tr, 1)

                def down(c, e, f, half, k_e):
                    n0 = first + c
                    pe.wait_ge(lo_ready, PER_E * e + n0 + 1)
                    if half == 0:
                        pe.wait_ge(e_lo, k_e + f + 1)
                    for k in range(2):
                        at = P * (2 * half + k)
                        hid = (eT_hi[:, at:at + P], eT_lo[:, at:at + P])
                        for o in range(2):
                            ins = three(bank[4 + o][:], hid, wt(n0, k, D, 512 * o, 512), f == 0 and half == 0 and k == 0,
                                        f == FSTEPS - 1 and half == 1 and k == 1)
                    ins.then_inc(w_used, 1)

                def scatter(e, q):
                    for o in range(2):
                        c = 2 * q + o
                        ins = pe.matmul(bank[7][:, 256 * o:256 * o + 256], y[:, P * c:P * c + P],
                                        wselT[:, bass.ds(e, 1), :].rearrange("p a b -> p (a b)"), start=True, stop=True)
                    ins.then_inc(y_sc, 1)

                pe.wait_ge(wt_ready, 4 * r + 4)
                gather(0)
                with pe.Fori(0, NE) as e:
                    k_e = FSTEPS * e + NE * FSTEPS * r
                    pe.wait_ge(he_lo_s, e + 9 * r + 1)
                    c = 0
                    for f in range(FSTEPS + 1):
                        bk = 2 * (f % 2)
                        if f < FSTEPS:
                            if f > 1:
                                pe.wait_ge(e_g, k_e + f - 1)
                            up(c, e, bank[bk][:])
                            up(c + 1, e, bank[bk][:])
                            c += 2
                        if f:
                            turn(f - 1, k_e)
                        if f == FSTEPS:
                            gather(e + 1)
                        if f < FSTEPS:
                            up(c, e, bank[bk + 1][:])
                            up(c + 1, e, bank[bk + 1][:])
                            c += 2
                        if f < 4:
                            if f == 0:
                                pe.wait_ge(y_ev, e + 9 * r + 1)
                            else:
                                pe.wait_ge(y_add, 4 * e + 36 * r + f + 1)
                            scatter(e, f)
                        if f:
                            down(c, e, f - 1, 0, k_e)
                            down(c + 1, e, f - 1, 1, k_e)
                            c += 2
                pe.wait_ge(y_ev, 9 * (r + 1))
                for q in range(4):
                    if q:
                        pe.wait_ge(y_add, 36 * r + 4 * NE + q + 1)
                    scatter(NE, q)
                pe.wait_ge(he_lo_s, 9 * (r + 1))

            experts(0)
            pe.wait_ge(count_ready, 1)
            most = pe.value_load(cntu[0:1, 0:1])
            with pe.If(most > SLOTS):
                experts(1)
            with pe.Else():
                pe.nop()
            norm_stat(6)
            pe.wait_ge(hf_ready, 14)
            for i in range(4):
                for k in range(4):
                    c = 4 * (i % 2) + k
                    ins = pe.transpose(bank[i][:, P * k:P * k + P], hf[:, c, P * (i // 2):P * (i // 2) + P], ident[:])
                ins.then_inc(fo_done, 1)


_OUT = ((1, 256, 1024), "float32")


def kernel(**inputs):
    import numpy as np
    import concourse.bacc as bacc
    from concourse.bass_utils import run_bass_kernel_spmd

    nc = bacc.Bacc("TRN2", target_bir_lowering=False, num_devices=1)
    names = ("x", "mem", "norm_mix_g", "w_in", "b_in", "a_conv_w", "a_conv_b", "a_ln_g", "a_ln_b", "a_w_out",
             "b_w_out", "c_conv_w", "c_w_out", "w_o", "norm_x_g", "norm_mem_g", "xq_w", "xk_w", "xv_w", "xo_w",
             "norm_ffn_g", "ffn_w1", "ffn_w3", "ffn_w2", "moe_router", "moe_w1", "moe_w3", "moe_w2", "final_g")
    arrays, args = {}, {}
    for name in names:
        a = np.ascontiguousarray(inputs[name])
        arrays[f"in_{name}"] = a
        args[name] = nc.dram_tensor(f"in_{name}", a.shape, mybir.dt.from_np(a.dtype), kind="ExternalInput").ap()
    args["out"] = nc.dram_tensor("out_0", _OUT[0], mybir.dt.from_np(np.dtype(_OUT[1])), kind="ExternalOutput").ap()
    trunk(nc, **args)
    r = run_bass_kernel_spmd(nc, [arrays], core_ids=[0])
    return r.results[0]["out_0"]
```

```python
import concourse.bass as bass
from concourse import mybir
from contextlib import ExitStack

F32 = mybir.dt.float32
F32R = mybir.dt.float32r
BF16 = mybir.dt.bfloat16
U32 = mybir.dt.uint32
I32 = mybir.dt.int32
ALU = mybir.AluOpType
ACT = mybir.ActivationFunctionType
AX = mybir.AxisListType

P = 128
D = 1024
S = 256
DB = D // P
TB = S // P
EPS = 1e-6
LAYERS = 2
AW = 512
AB = AW // P
KA, KC = 31, 3
GROUPS, HEADS, DH = 3, 4, 64
XH = 4
FF = 2816
FFB = FF // 256
NE, EFF = 8, 3584
FSTEPS = EFF // 512
SLOTS = 128
RAW, SPLIT = 6, 3
CW = 2048
NEG = -1e30

PLAN = [("agate", 0), ("aval", 0), ("agate", 1), ("aval", 1)]
PLAN += [(k, i) for k in "qkv" for i in range(3)]
PLAN += [("cb", 0), ("cb", 1), ("cc", 0), ("ch", 0), ("cc", 1), ("ch", 1)]
PLAN += [("gc", i) for i in range(4)] + [("cout", 0), ("cout", 1), ("bout", 0), ("bout", 1)]
PLAN += [("gb", i) for i in range(4)] + [("ga", 0), ("ga", 1), ("aout", 0), ("aout", 1), ("ga", 2), ("ga", 3)]
PLAN += [("xk", 0)] + [("wo", i) for i in range(4)] + [("xk", i) for i in (1, 2, 3)]
PLAN += [(k, i) for k in ("xq", "xv", "xo") for i in range(4)]
AT = {what: c for c, what in enumerate(PLAN)}
IN_BLOCK = {"aval": 0, "agate": 2, "q": 4, "k": 7, "v": 10, "cb": 13, "cc": 15, "ch": 17, "ga": 19, "gb": 23, "gc": 27}
C_FFN = len(PLAN)
HEAD_AT = [10, 13, 16, 19]
OT_AT = 23
CONV_C_AT = {17: (0, 1), 20: (2, 3)}
C_AT = 21
LN_AT = (29, 31)
MEM_AT = (34, 35)
CONV_A_AT = dict(zip(range(3, 29), (5, 7, 7, 7, 7, 7, 7, 0, 5, 5, 0, 7, 7, 0, 1, 5, 0, 1, 2, 6, 6, 7, 7, 7, 7, 4)))
BASE = [0, 57 + 3 * FFB]
WT_BANK, FINAL_BANK = (0, 1, 4, 5), (2, 3, 7, 0)
MOE = BASE[1] + 57
PER_E = 6 * FSTEPS
EXTRAS = 3
EXTRA = MOE + NE * PER_E - EXTRAS
SUMMED = (1, 2, 4, 5)
G_MIX, G_X, G_MEM, G_FFN, A_CB, A_LG, A_LB, C_CW = 0, 16, 32, 48, 64, 72, 80, 88


def trunk(nc, x, mem, norm_mix_g, w_in, b_in, a_conv_w, a_conv_b, a_ln_g, a_ln_b, a_w_out, b_w_out,
          c_conv_w, c_w_out, w_o, norm_x_g, norm_mem_g, xq_w, xk_w, xv_w, xo_w, norm_ffn_g, ffn_w1,
          ffn_w3, ffn_w2, moe_router, moe_w1, moe_w3, moe_w2, final_g, out):
    with ExitStack() as ctx:
        def sb(name, shape, dt=F32):
            return ctx.enter_context(nc.sbuf_tensor(name, shape, dt))

        def sem(name):
            return ctx.enter_context(nc.semaphore(name))

        raw = sb("raw", [P, RAW, CW])
        whi = sb("whi", [P, SPLIT, CW], F32R)
        wlo = sb("wlo", [P, SPLIT, CW], F32R)
        h_hl = sb("h_hl", [P, 2, DB, S], F32R)
        act_hl = sb("act_hl", [P, 4096], F32R)
        xT = sb("xT", [P, DB, S])
        memhat = sb("memhat", [P, DB, S])
        U = sb("U", [P, 14720])
        par = sb("par", [P, 4, P])
        ident = sb("ident", [P, P])
        ones = sb("ones", [P, P])
        mask = sb("mask", [P, GROUPS, S], BF16)
        rstd = sb("rstd", [P, S])
        router = sb("router", [P, DB, NE])
        small = sb("small", [P, 36])
        bank = [ctx.enter_context(nc.psum_tensor(f"bank{i}", [P, 512], F32)) for i in range(8)]

        def u(at, *shape):
            size = 1
            for s_ in shape:
                size *= s_
            ap = U[:, at:at + size]
            if len(shape) == 2:
                return ap.rearrange("p (a b) -> p a b", a=shape[0])
            if len(shape) == 3:
                return ap.rearrange("p (a b c) -> p a b c", a=shape[0], b=shape[1])
            return ap

        def v(at, *shape):
            size = 1
            for s_ in shape:
                size *= s_
            ap = act_hl[:, at:at + size]
            return ap.rearrange("p (a b) -> p a b", a=shape[0]) if len(shape) == 2 else ap

        sq, hf = u(0, DB, S), u(2048, DB, S)
        qT, kT = u(0, 6, S), u(1536, 6, S)
        vtok = u(3072, TB, GROUPS * HEADS * DH)
        apad = u(4608, AB, KA - 1 + S)
        sg = u(9856, 2, 2, S)
        aacc, agate = u(5752, AB, S), u(5752, AB, S)
        cb = u(6776, AB, S)
        cpad = u(7800, AB, KC - 1 + S)
        cacc, ccv, asq = u(8832, AB, S), u(8832, AB, S), u(8832, AB, S)
        Y = u(6776, DB, S)
        prob0, prob1 = u(9856, GROUPS, P), u(9856 + 384, GROUPS, S)
        pT0, pT1 = u(11008, GROUPS, P), u(11008 + 384, GROUPS, S)
        otok = u(12160, TB, HEADS * DH)
        merged = u(12672, DB, S)
        vbias = u(12672, GROUPS * HEADS * DH)
        c_hi, c_lo = v(0, AB, S), v(1024, AB, S)
        a_hi, a_lo = v(2048, AB, S), v(3072, AB, S)
        o_hi, o_lo = v(2048, 2, S), v(2560, 2, S)
        kx, qx = u(4096, DB, S), u(6144, DB, S)
        vx = u(8192, TB, D)
        probx = u(10240, XH * TB, S)
        pTx = u(12288, XH * TB, S)
        m_hi, m_lo = v(0, DB, S), v(2048, DB, S)
        sil, gf = u(4096, 2, 512), u(5120, 2, 512)
        g_hi, g_lo = v(0, 2, 512), v(1024, 2, 512)
        zerosf = u(6144, 256)
        zeros = zerosf.bitcast(BF16)
        htok = u(4096, TB, D)
        sel = u(6144, TB, NE, SLOTS)
        wsel = u(8448, TB, NE, SLOTS)
        esil, eg = u(8448, 2, 512), u(9472, 512)
        wselT = u(10496, NE + 1, S)
        lgT = U[0:NE, 10752:11008]
        y = u(12800, D)
        rt = U[:, 13824:14720]
        iota = rt[:, 0:128]
        strict = rt[:, 128:256]
        allone = rt[:, 256:384]
        lg, top, idxf, oh0, oh1, msk, comb, posm, posr = (
            rt[:, 448 + 16 * i:464 + 16 * i].rearrange("p (b e) -> p b e", e=NE) for i in range(9))
        idxu = sb("idxu", [P, TB, NE], U32)
        wts = rt[:, 592:608]
        cntf = rt[:, 608:609]
        iota8 = rt[:, 616:624]
        cntu = sb("cntu", [P, 1], U32)
        eT_hi, eT_lo = v(0, 512), v(512, 512)
        he_hi, he_lo = v(2048, D), v(3072, D)
        xin = u(4096, TB, D)
        min_ = memhat[:].rearrange("p a b -> p (a b)").rearrange("p (t d) -> p t d", t=TB)
        msq = u(9856, DB, S)
        prow = u(8192, 4, P)
        dist = U[:, 8704:8960].bitcast(I32)
        rest = U[:, 8960:9216].bitcast(I32)
        ban = u(9216, 2, S)
        yout = u(4096, TB, D)
        gfin = u(6144, D)
        fsq = u(2048, 4, 512)

        extra = [memhat[:].rearrange("p a b -> p (a b)"), U[:, 0:2048], U[:, 2048:4096]]

        w_raw = [sem(f"w_raw{i}") for i in range(RAW)]
        w_extra = [sem(f"w_extra{i}") for i in range(EXTRAS)]
        hi_ready = sem("hi_ready")
        lo_ready = sem("lo_ready")
        w_used = sem("w_used")
        in_par, in_x, in_mem, in_vb, in_rt = (sem(s_) for s_ in ("in_par", "in_x", "in_mem", "in_vb", "in_rt"))
        const = sem("const")
        rt_const = sem("rt_const")
        tr_done = sem("tr_done")
        par_ready = sem("par_ready")
        x_ready = sem("x_ready")
        mT_ready = sem("mT_ready")
        msq_ready, mss_done, mrt_ready = sem("msq_ready"), sem("mss_done"), sem("mrt_ready")
        sq_ready = sem("sq_ready")
        sq_sum, msq_sum = sem("sq_sum"), sem("msq_sum")
        ss_done = sem("ss_done")
        rt_ready = sem("rt_ready")
        hf_ready = sem("hf_ready")
        h_hi_s = sem("h_hi_s")
        h_lo_s = sem("h_lo_s")
        mf_ready, m_hi_s, m_lo_s = sem("mf_ready"), sem("m_hi_s"), sem("m_lo_s")
        out_act = sem("out_act")
        out_dve = sem("out_dve")
        gated = sem("gated")
        product = sem("product")
        pads = sem("pads")
        conv_a, conv_c = sem("conv_a"), sem("conv_c")
        c_f, c_hi_s, c_lo_s = sem("c_f"), sem("c_hi_s"), sem("c_lo_s")
        ln_st = sem("ln_st")
        ln_xc, ln_sq, ln_rt, ln_y = (sem(s_) for s_ in ("ln_xc", "ln_sq", "ln_rt", "ln_y"))
        a_f, a_hi_s, a_lo_s = sem("a_f"), sem("a_hi_s"), sem("a_lo_s")
        sc_done, mx_ready, pr_ready, pt_done, pT_ready, pv_done, o_ready = (
            sem(s_) for s_ in ("sc_done", "mx_ready", "pr_ready", "pt_done", "pT_ready", "pv_done", "o_ready"))
        oT_done, o_hi_s, o_lo_s = sem("oT_done"), sem("o_hi_s"), sem("o_lo_s")
        mg_hi_s, mg_lo_s = sem("mg_hi_s"), sem("mg_lo_s")
        xs_done, xm_ready, xp_ready, xn_ready, xpt_done, xpT_ready, xpv_done, xo_hi_s, xo_lo_s = (
            sem(s_) for s_ in ("xs_done", "xm_ready", "xp_ready", "xn_ready", "xpt_done", "xpT_ready",
                               "xpv_done", "xo_hi_s", "xo_lo_s"))
        z_ready = sem("z_ready")
        silu_s, g_s, g_hi_s, g_lo_s = sem("silu_s"), sem("g_s"), sem("g_hi_s"), sem("g_lo_s")
        lt_ready, lt_done = sem("lt_ready"), sem("lt_done")
        rl_done, ht_done, ht_ready, rl_ready, re_ready, route = (
            sem(s_) for s_ in ("rl_done", "ht_done", "ht_ready", "rl_ready", "re_ready", "route"))
        mk_ready, cnt_done, count_ready, sel0_ready, sel_ready, wt_done, wt_ready = (
            sem(s_) for s_ in ("mk_ready", "cnt_done", "count_ready", "sel0_ready", "sel_ready", "wt_done", "wt_ready"))
        ga_done, he_hi_s, he_lo_s, e_silu, e_g, e_tr, e_hi, e_lo, y_ev, y_sc, y_add = (
            sem(s_) for s_ in ("ga_done", "he_hi_s", "he_lo_s", "e_silu", "e_g", "e_tr", "e_hi",
                               "e_lo", "y_ev", "y_sc", "y_add"))
        y_half = sem("y_half")
        wt_kept = sem("wt_kept")
        in_fin = sem("in_fin")
        fo_done, fo_sq, fo_ms, fo_rt, fo_ready, out_sent = (
            sem(s_) for s_ in ("fo_done", "fo_sq", "fo_ms", "fo_rt", "fo_ready", "out_sent"))
        dve_own = sem("dve_own")
        round_own = sem("round_own")

        block = ctx.enter_context(nc.Block())

        def local(n):
            lay = int(n >= BASE[1])
            return lay, n - BASE[lay]

        def kind(n):
            return PLAN[local(n)[1]][0]

        def slot(n, r):
            return (n - EXTRAS * r) % RAW, (n - EXTRAS * r) // RAW + 1

        def landed(n):
            if EXTRA <= n < EXTRA + EXTRAS:
                return extra[n - EXTRA], w_extra[n - EXTRA], 16
            at, times = slot(n, int(n > EXTRA))
            return raw[:, at, :], w_raw[at], 16 * times

        def used_words(n):
            return 1024 if local(n)[1] < len(PLAN) and kind(n) == "bout" else CW

        def by_vector(n):
            return kind(n) in ("aval", "ch", "v")

        def taken(n):
            lay, c = local(n)
            if kind(n) in ("wo", "xo"):
                return x_ready, 12 * lay + (4 if kind(n) == "wo" else 8) + PLAN[c][1] + 1
            dense = [BASE[i] + k for i in range(LAYERS) for k in range(C_FFN) if PLAN[k][0] not in ("wo", "xo")]
            mine = by_vector(n)
            return (out_dve if mine else out_act), sum(1 for m in dense if m <= n and by_vector(m) == mine)

        def norm_bank(q):
            return bank[3 if q == 3 else 7]

        def ln_bank(n):
            return 2 * (n % 2) + 1

        @block.sync
        def _(sp):
            def load(slot, value, dst_words, pattern, src, wait=None):
                if wait is not None:
                    sp.wait_ge(lo_ready, wait)
                sp.dma_start(raw[:, slot, 0:dst_words].rearrange(pattern[0], **pattern[1]), src)\
                  .then_inc(w_raw[slot], 16)

            def k8(w, block_):
                return w.rearrange("(k p) n -> p k n", p=P)[:, :, 256 * block_:256 * block_ + 256]

            def dense(n, src, k):
                load(n % RAW, 0, k * src.shape[2], ("p (k n) -> p k n", {"k": k}), src,
                     n - RAW + 1 if n >= RAW else None)

            for t in range(TB):
                sp.dma_start(xin[:, t, :], x[0, P * t:P * t + P, :]).then_inc(in_x, 16)
            sp.wait_ge(in_par, 11 * 16)
            for lay in range(LAYERS):
                b = BASE[lay]
                for c, (what, i) in enumerate(PLAN):
                    n = b + c
                    if c == RAW:
                        if lay == 0:
                            sp.dma_start(min_, mem[0].rearrange("(b p) d -> p b d", p=P)).then_inc(in_mem, 16)
                            sp.dma_start(router[:], moe_router[0].rearrange("(k p) e -> p k e", p=P)).then_inc(in_rt, 16)
                        else:
                            sp.wait_ge(hf_ready, 16)
                        sp.dma_start(vbias, b_in[lay:lay + 1, 2560:3328].to_broadcast([P, 768])).then_inc(in_vb, 16)
                    if what in IN_BLOCK:
                        dense(n, k8(w_in[lay], IN_BLOCK[what] + i), 8)
                    elif what in ("cout", "bout", "aout"):
                        w = {"cout": c_w_out, "bout": b_w_out, "aout": a_w_out}[what][lay]
                        k = w.shape[0] // P
                        dense(n, w.rearrange("(k p) n -> p k n", p=P)[:, :, 512 * i:512 * i + 512], k)
                    else:
                        w = {"wo": w_o, "xk": xk_w, "xq": xq_w, "xv": xv_w, "xo": xo_w}[what]
                        dense(n, k8(w[lay], i), 8)
                if lay == 0:
                    f = b + C_FFN
                    w1v, w3v = (w[0].rearrange("(k p) n -> p k n", p=P) for w in (ffn_w1, ffn_w3))
                    w2v = ffn_w2[0].rearrange("(k p) n -> p k n", p=P)
                    dense(f, w1v[:, :, 0:256], 8)
                    dense(f + 1, w3v[:, :, 0:256], 8)
                    with sp.Fori(0, (FFB - 1) // 2) as i:
                        for c in range(6):
                            n0 = f + 2 + c
                            j = 1 + c // 3
                            if c % 3 < 2:
                                src = (w1v, w3v)[c % 3][:, :, bass.ds(512 * i + 256 * j, 256)]
                                k = 8
                            else:
                                src = w2v[:, bass.ds(4 * i + 2 * (j - 1), 2), :]
                                k = 2
                            load(n0 % RAW, 0, CW, ("p (k n) -> p k n", {"k": k}), src, 6 * i + n0 - RAW + 1)
                    dense(f + 3 * FFB - 1, w2v[:, 2 * FFB - 2:2 * FFB, :], 2)

            ew1, ew3 = (w[0].rearrange("e (k p) n -> e p k n", p=P) for w in (moe_w1, moe_w3))
            ew2 = moe_w2[0].rearrange("e (k p) n -> e p k n", p=P)

            def experts(r):
                first = MOE + NE * PER_E * r

                def fetch(e, c, k, src):
                    if isinstance(e, int):
                        n = first + PER_E * e + c
                        dst, done, _ = landed(n)
                        if n < EXTRA:
                            sp.wait_ge(lo_ready, n - RAW + 1)
                    else:
                        at, _ = slot(first + c, r)
                        dst, done = raw[:, at, :], w_raw[at]
                        sp.wait_ge(lo_ready, PER_E * e + first + c - RAW + 1)
                    sp.dma_start(dst.rearrange("p (k n) -> p k n", k=k), src).then_inc(done, 16)

                def up(w, e, f, half, c):
                    fetch(e, c, 4, w[bass.ds(e, 1), :, 4 * half:4 * half + 4, 512 * f:512 * f + 512]
                          .rearrange("e p k n -> p (e k) n"))

                def down(e, f, half, c):
                    fetch(e, c, 2, ew2[bass.ds(e, 1), :, 4 * f + 2 * half:4 * f + 2 * half + 2, :]
                          .rearrange("e p k n -> p (e k) n"))

                def ahead():
                    c = PER_E - EXTRAS
                    sp.wait_ge(m_hi_s, 4)
                    sp.wait_ge(m_lo_s, 4)
                    down(NE - 1, FSTEPS - 2, 1, c)
                    sp.wait_ge(ss_done, 6)
                    down(NE - 1, FSTEPS - 1, 0, c + 1)
                    sp.wait_ge(ht_done, 4)
                    down(NE - 1, FSTEPS - 1, 1, c + 2)

                def expert(e, count=PER_E, ahead_of=None):
                    c = 0
                    for f in range(FSTEPS + 1):
                        if f < FSTEPS:
                            for w in (ew1, ew3):
                                for half in range(2):
                                    up(w, e, f, half, c)
                                    c += 1
                        if f:
                            for half in range(2):
                                if ahead_of == c:
                                    ahead()
                                if c < count:
                                    down(e, f - 1, half, c)
                                c += 1

                if r == 0:
                    expert(0, ahead_of=SPLIT + RAW)
                    with sp.Fori(1, NE - 1) as e:
                        expert(e)
                    expert(NE - 1, PER_E - EXTRAS)
                else:
                    with sp.Fori(0, NE) as e:
                        expert(e)

            experts(0)
            sp.wait_ge(count_ready, 1)
            most = sp.value_load(cntu[0:1, 0:1])
            with sp.If(most > SLOTS):
                experts(1)
                sp.wait_ge(he_lo_s, 2 * NE)
            with sp.Else():
                sp.nop()
            sp.wait_ge(he_lo_s, NE)
            sp.dma_start(gfin, final_g.rearrange("(a d) -> a d", a=1).to_broadcast([P, D])).then_inc(in_fin, 16)
            for b in range(TB):
                for i in range(2):
                    sp.wait_ge(fo_ready, 2 * b + i + 1)
                    sp.dma_start(out[0, b * P:(b + 1) * P, 512 * i:512 * i + 512],
                                 yout[:, b, 512 * i:512 * i + 512]).then_inc(out_sent, 16)
            sp.wait_ge(out_sent, 64)

        @block.gpsimd
        def _(gp):
            gp.memset(small[:, 32:33], EPS).then_inc(const, 1)
            gp.memset(ident[:], 0.0).then_inc(const, 1)
            gp.memset(ones[:], 1.0 / D).then_inc(const, 1)
            gp.iota(dist, pattern=[[-1, S]], base=P, channel_multiplier=1).then_inc(const, 1)
            gp.wait_ge(const, 4)
            gp.affine_select(out=ident[:], in_=ident[:], compare_op=ALU.not_equal, fill=1.0, base=0,
                             pattern=[[-1, P]], channel_multiplier=1).then_inc(const, 1)

            for lay in range(LAYERS):
                b = BASE[lay]
                if lay:
                    gp.wait_ge(h_lo_s, 16)
                else:
                    gp.wait_ge(tr_done, 5)
                gp.memset(apad[:, :, 0:KA - 1], 0.0).then_inc(pads, 1)
                gp.memset(cpad[:, :, 0:KC - 1], 0.0).then_inc(pads, 1)
                if lay == 0:
                    for k in range(4):
                        gp.wait_ge(msq_ready, k + 1)
                        gp.tensor_tensor(msq[:, 2 * k, :], msq[:, 2 * k, :], msq[:, 2 * k + 1, :], ALU.add).then_inc(msq_sum, 1)
                for branch, (out_, gate) in enumerate((("cout", "gc"), ("bout", "gb"), ("aout", "ga"))):
                    for i in range(4):
                        later = max(AT[out_, i // 2], AT[gate, i])
                        s_, val = taken(b + later)
                        gp.wait_ge(s_, val)
                        yb, mb, gb = Y[:, 2 * i:2 * i + 2, :], merged[:, 2 * i:2 * i + 2, :], sg[:, i % 2, :, :]
                        if branch == 0:
                            gp.tensor_tensor(mb, mb, yb, ALU.mult).then_inc(gated, 1)
                        else:
                            gp.tensor_tensor(yb, gb, yb, ALU.mult).then_inc(product, 1)
                            gp.wait_ge(product, 8 * lay + 4 * (branch - 1) + i + 1)
                            gp.tensor_tensor(mb, mb, yb, ALU.add).then_inc(gated, 1)
                for q in (3 * lay + 1, 3 * lay + 2):
                    sums = 5 * SUMMED.index(q)
                    for pair in range(3):
                        gp.wait_ge(sq_ready, 4 * q + pair + 1)
                        gp.tensor_tensor(sq[:, 2 * pair, :], sq[:, 2 * pair, :], sq[:, 2 * pair + 1, :], ALU.add)\
                          .then_inc(sq_sum, 1)
                        if pair:
                            gp.wait_ge(sq_sum, sums + 2 * pair)
                            gp.tensor_tensor(sq[:, 0, :], sq[:, 0, :], sq[:, 2 * pair, :], ALU.add).then_inc(sq_sum, 1)

            gp.wait_ge(hf_ready, 24)
            gp.iota(iota, pattern=[[1, P]], base=0, channel_multiplier=0,
                    allow_small_or_imprecise_dtypes=True).then_inc(rt_const, 1)
            gp.iota(iota8, pattern=[[1, NE]], base=0, channel_multiplier=0,
                    allow_small_or_imprecise_dtypes=True).then_inc(rt_const, 1)
            gp.memset(allone, 1.0).then_inc(rt_const, 1)
            gp.wait_ge(rt_const, 3)
            gp.affine_select(out=strict, in_=allone, compare_op=ALU.is_gt, fill=0.0, base=0,
                             pattern=[[1, P]], channel_multiplier=-1).then_inc(rt_const, 1)
            gp.memset(wselT[:, 0, :], 0.0).then_inc(rt_const, 1)
            gp.memset(y, 0.0).then_inc(y_ev, 1)

        @block.scalar
        def _(act):
            def split_at(src, arrived, value, n, used, words=CW):
                act.wait_ge(arrived, value)
                if used is not None:
                    act.wait_ge(w_used, used)
                act.activation(whi[:, n % SPLIT, 0:words], src[:, 0:words], ACT.Copy).then_inc(hi_ready, 1)

            def split(n):
                split_at(*landed(n), n, n - SPLIT + 1 if n >= SPLIT else None, used_words(n))

            def squares(q, pair):
                act.wait_ge(x_ready, 4 * q + pair + 1)
                if q and pair == 0:
                    act.wait_ge(ss_done, q)
                act.activation(sq[:, 2 * pair:2 * pair + 2, :], xT[:, 2 * pair:2 * pair + 2, :],
                               ACT.Square).then_inc(sq_ready, 1)

            def before_root():
                act.activation(small[:, 33:34], small[:, 32:33], ACT.Sqrt)

            def root(q):
                act.wait_ge(ss_done, q + 1)
                act.activation(rstd[:], norm_bank(q)[:, 0:256], ACT.Sqrt, bias=small[:, 32:33]).then_inc(rt_ready, 1)

            def norm_hi(q):
                for pair in range(4):
                    act.wait_ge(hf_ready, 4 * q + pair + 1)
                    act.activation(h_hl[:, 0, 2 * pair:2 * pair + 2, :], hf[:, 2 * pair:2 * pair + 2, :],
                                   ACT.Copy).then_inc(h_hi_s, 1)

            act.dma_start(prow[0:124, 0, :], b_in.rearrange("l (c p) -> (l c) p", p=P)).then_inc(in_par, 16)
            for i in range(2):
                act.dma_start(prow[0:124, 1 + i, :],
                              a_conv_w[i, :, :].rearrange("k (c p) -> (k c) p", p=P)).then_inc(in_par, 16)
            for at, src in ((G_MIX, norm_mix_g), (G_X, norm_x_g), (G_MEM, norm_mem_g), (G_FFN, norm_ffn_g),
                            (A_CB, a_conv_b), (A_LG, a_ln_g), (A_LB, a_ln_b)):
                m = src.shape[0] * src.shape[1] // P
                act.dma_start(prow[at:at + m, 3, :], src.rearrange("l (c p) -> (l c) p", p=P)).then_inc(in_par, 16)
            act.dma_start(prow[C_CW:C_CW + 24, 3, :],
                          c_conv_w.rearrange("l k (c p) -> (l k c) p", p=P)).then_inc(in_par, 16)

            act.wait_ge(const, 4)
            before_root()
            for i in range(4):
                squares(0, i)
            act.wait_ge(tr_done, 5)
            act.activation(par[:, 0:3, 0:124], bank[0][:, 0:384].rearrange("p (a b) -> p a b", a=3)[:, :, 0:124], ACT.Copy)
            act.activation(par[:, 3, 0:112], bank[0][:, 384:496], ACT.Copy).then_inc(par_ready, 1)
            root(0)
            split(0)
            split(1)
            norm_hi(0)
            split(2)

            def bias(lay, cblock):
                return par[:, 0, 62 * lay + cblock:62 * lay + cblock + 1]

            def take(n, dst, func, lay, block_):
                src = bank[2 * (n % 2)]
                for i in range(2):
                    ins = act.activation(dst[i], src[:, 256 * i:256 * i + 256], func,
                                         bias=bias(lay, 2 * block_ + i))
                ins.then_inc(out_act, 1)

            def head_exp(lay, h):
                k = 4 * lay + h
                act.wait_ge(mx_ready, k + 1)
                if k:
                    act.wait_ge(o_ready, k)
                act.activation(prob0, prob0, ACT.Exp, bias=small[:, 0:1], accum_out=small[:, 4:5])
                act.activation(prob1, prob1, ACT.Exp, bias=small[:, 1:2], accum_out=small[:, 5:6])\
                   .then_inc(pr_ready, 1)

            def head_pT(lay, h):
                act.wait_ge(pt_done, 4 * lay + h + 1)
                act.activation(pT0, bank[4][:, 0:384].rearrange("p (a b) -> p a b", a=3), ACT.Copy)
                act.activation(pT1[:, 0:2, :], bank[5][:].rearrange("p (a b) -> p a b", a=2), ACT.Copy)
                act.activation(pT1[:, 2, :], bank[6][:, 0:256], ACT.Copy).then_inc(pT_ready, 1)

            def post(n):
                lay, c = local(n)
                b = BASE[lay]
                what, i = PLAN[c]
                act.wait_ge(w_used, n + 1)
                if what in IN_BLOCK:
                    blk = IN_BLOCK[what] + i
                if what == "agate":
                    take(n, [agate[:, 2 * i + k, :] for k in range(2)], ACT.Sigmoid, lay, blk)
                elif what in ("cb", "cc"):
                    dst = cb if what == "cb" else ccv
                    take(n, [dst[:, 2 * i + k, :] for k in range(2)], ACT.Identity, lay, blk)
                elif what in ("q", "k"):
                    dst = qT if what == "q" else kT
                    take(n, [dst[:, 2 * i + k, :] for k in range(2)], ACT.Identity, lay, blk)
                elif what in ("cout", "bout", "aout"):
                    if what != "cout":
                        act.wait_ge(gated, 12 * lay + (0 if what == "bout" else 4) + 2 * (i + 1))
                    for k in range(2):
                        ins = act.activation(Y[:, 4 * i + 2 * k:4 * i + 2 * k + 2, :],
                                             bank[2 * (n % 2) + k][:].rearrange("p (a b) -> p a b", a=2), ACT.Copy)
                    ins.then_inc(out_act, 1)
                elif what == "gc":
                    take(n, [merged[:, 2 * i + k, :] for k in range(2)], ACT.Sigmoid, lay, blk)
                elif what in ("gb", "ga"):
                    j = i + (0 if what == "gb" else 4)
                    if j >= 2:
                        act.wait_ge(gated, 12 * lay + 4 + j - 1)
                    take(n, [sg[:, i % 2, k, :] for k in range(2)], ACT.Sigmoid, lay, blk)
                elif what in ("xk", "xq", "xv"):
                    src = bank[2 * (n % 2)][:].rearrange("p (a b) -> p a b", a=2)
                    dst = {"xk": kx[:, 2 * i:2 * i + 2, :], "xq": qx[:, 2 * i:2 * i + 2, :],
                           "xv": vx[:, :, 256 * i:256 * i + 256]}[what]
                    act.activation(dst, src, ACT.Copy).then_inc(out_act, 1)
                elif what == "wo":
                    squares(3 * lay + 1, i)
                elif what == "xo":
                    squares(3 * lay + 2, i)
                if n == 0:
                    act.wait_ge(tr_done, 9)
                    for k in range(4):
                        act.activation(memhat[:, 2 * k:2 * k + 2, :], bank[4 + k][:].rearrange("p (a b) -> p a b", a=2),
                                       ACT.Copy).then_inc(mT_ready, 1)
                    for k in range(4):
                        act.wait_ge(mT_ready, k + 1)
                        act.activation(msq[:, 2 * k:2 * k + 2, :], memhat[:, 2 * k:2 * k + 2, :],
                                       ACT.Square).then_inc(msq_ready, 1)
                if n == 2:
                    act.wait_ge(mss_done, 1)
                    act.activation(rstd[:], bank[7][:, 0:256], ACT.Sqrt, bias=small[:, 32:33]).then_inc(mrt_ready, 1)
                if c == C_AT:
                    act.wait_ge(c_f, lay + 1)
                    act.activation(c_hi, cacc, ACT.Copy).then_inc(c_hi_s, 1)
                if c == LN_AT[0]:
                    act.wait_ge(ln_xc, lay + 1)
                    act.activation(asq, aacc, ACT.Square).then_inc(ln_sq, 1)
                if c == LN_AT[1]:
                    act.wait_ge(ln_st, 2 * lay + 2)
                    act.activation(rstd[:], bank[ln_bank(b + LN_AT[1] + 1)][:, 0:256], ACT.Sqrt, scale=float(D) / AW,
                                   bias=small[:, 32:33]).then_inc(ln_rt, 1)
                    act.wait_ge(ln_y, lay + 1)
                    for k in range(AB):
                        ins = act.activation(asq[:, k, :], aacc[:, k, :], ACT.Silu,
                                             scale=par[:, 3, A_LG + 4 * lay + k:A_LG + 4 * lay + k + 1],
                                             bias=par[:, 3, A_LB + 4 * lay + k:A_LB + 4 * lay + k + 1])
                    ins.then_inc(a_f, 1)
                    act.wait_ge(a_f, lay + 1)
                    act.activation(a_hi, asq, ACT.Copy).then_inc(a_hi_s, 1)
                for h in range(HEADS):
                    if c == HEAD_AT[h] + 2:
                        head_pT(lay, h)
                for h in range(HEADS):
                    if c == HEAD_AT[h]:
                        head_exp(lay, h)
                if c == OT_AT:
                    act.wait_ge(oT_done, lay + 1)
                    act.activation(o_hi, bank[4][:].rearrange("p (a b) -> p a b", a=2), ACT.Copy).then_inc(o_hi_s, 1)
                if c == MEM_AT[1]:
                    for half in range(2):
                        act.wait_ge(mf_ready, 2 * lay + half + 1)
                        act.activation(m_hi[:, 4 * half:4 * half + 4, :], hf[:, 4 * half:4 * half + 4, :],
                                       ACT.Copy).then_inc(m_hi_s, 1)
                if c == AT["ga", 3]:
                    for pair in range(4):
                        act.wait_ge(gated, 12 * lay + 8 + pair + 1)
                        act.activation(h_hl[:, 0, 2 * pair:2 * pair + 2, :], merged[:, 2 * pair:2 * pair + 2, :],
                                       ACT.Copy).then_inc(mg_hi_s, 1)
                if c == AT["wo", 3]:
                    before_root()
                if c == AT["wo", 3] + 1:
                    root(3 * lay + 1)
                    norm_hi(3 * lay + 1)
                if c == AT["xv", 0]:
                    for i in range(XH * TB):
                        act.wait_ge(xm_ready, 8 * lay + i + 1)
                        act.activation(probx[:, i, :], bank[4 + i // 2][:, 256 * (i % 2):256 * (i % 2) + 256],
                                       ACT.Exp, scale=1.0 / 16, bias=small[:, 8 + i:9 + i],
                                       accum_out=small[:, 16 + i:17 + i]).then_inc(xp_ready, 1)
                if c == AT["xv", 2]:
                    for i in range(4):
                        act.wait_ge(xpt_done, 4 * lay + i + 1)
                        act.activation(pTx[:, 2 * i:2 * i + 2, :], bank[4 + i][:].rearrange("p (a b) -> p a b", a=2),
                                       ACT.Copy).then_inc(xpT_ready, 1)
                if c == AT["xv", 3]:
                    for i in range(4):
                        act.wait_ge(xpv_done, 4 * lay + i + 1)
                        act.activation(h_hl[:, 0, 2 * i:2 * i + 2, :], bank[4 + i][:].rearrange("p (a b) -> p a b", a=2),
                                       ACT.Copy).then_inc(xo_hi_s, 1)
                if c == AT["xo", 3]:
                    before_root()
                    root(3 * lay + 2)
                    if lay == 0:
                        norm_hi(2)

            def ffn_act(i, j, f0):
                act.wait_ge(w_used, f0)
                act.activation(sil[:, j, :], bank[2 * j][:], ACT.Silu).then_inc(silu_s, 1)
                act.wait_ge(g_s, i + 1)
                act.activation(g_hi[:, j, :], gf[:, j, :], ACT.Copy).then_inc(g_hi_s, 1)

            for lay in range(LAYERS):
                b = BASE[lay]
                for n in range(b + SPLIT, b + C_FFN):
                    post(n - SPLIT)
                    split(n)
                if lay == 0:
                    f = b + C_FFN
                    for k in range(3):
                        post(f - 3 + k)
                        if k < 2:
                            split(f + k)
                    with act.Fori(0, (FFB - 1) // 2) as i:
                        for c in range(6):
                            n0 = f + 2 + c
                            if c == 2:
                                ffn_act(2 * i, 0, 6 * i + f + 2)
                            if c == 4:
                                ffn_act(2 * i + 1, 1, 6 * i + n0 - 2)
                            split_at(raw[:, n0 % RAW, :], w_raw[n0 % RAW], 16 * i + 16 * (n0 // RAW + 1), n0,
                                     6 * i + n0 - SPLIT + 1)
                    split(f + 3 * FFB - 1)
                    ffn_act(FFB - 1, 0, f + 3 * FFB - 2)
                    split(BASE[1])
                    split(BASE[1] + 1)
                    for i in range(4):
                        squares(3, i)
                    before_root()
                    root(3)
                    norm_hi(3)
                    split(BASE[1] + 2)
                else:
                    for n in range(MOE - SPLIT, MOE):
                        post(n)
                        split(n + SPLIT)

            act.activation(small[:, 34:35], small[:, 32:33], ACT.Exp)
            for i in range(4):
                act.wait_ge(ht_done, i + 1)
                act.activation(htok[:, i // 2, 512 * (i % 2):512 * (i % 2) + 512], bank[i][:], ACT.Copy)\
                   .then_inc(ht_ready, 1)
                if i == 1:
                    act.wait_ge(rl_ready, 1)
                    act.activation(wts[:, 2:4], wts[:, 0:2], ACT.Exp).then_inc(re_ready, 1)
            act.activation(small[:, 35:36], small[:, 32:33], ACT.Silu)

            def experts(r):
                first = MOE + NE * PER_E * r
                def gathered(count):
                    act.wait_ge(ga_done, count)
                    for k in range(2):
                        ins = act.activation(he_hi[:, 512 * k:512 * k + 512], bank[2 + k][:], ACT.Copy)
                    ins.then_inc(he_hi_s, 1)

                def transposed(count):
                    act.wait_ge(e_tr, count)
                    act.activation(eT_hi, bank[6][:], ACT.Copy).then_inc(e_hi, 1)

                if r:
                    for c in range(SPLIT):
                        split(first + c)
                    act.activation(wselT[:, 0, :], wselT[:, NE, :], ACT.Copy).then_inc(wt_kept, 1)
                    act.wait_ge(wt_kept, 1)
                gathered(8 * r + 1)
                for i in range(4):
                    act.wait_ge(wt_done, 4 * r + i + 1)
                    act.activation(wselT[:, 1 + 2 * i:3 + 2 * i, :], bank[WT_BANK[i]][:].rearrange("p (a b) -> p a b", a=2),
                                   ACT.Copy).then_inc(wt_ready, 1)

                def body(e, last):
                    n_e = PER_E * e + first
                    k_e = FSTEPS * e + NE * FSTEPS * r
                    for c in range(SPLIT, PER_E + SPLIT):
                        for f in range(FSTEPS):
                            w1b = 1 if f == 0 else 6 * f - 1
                            if c == w1b + SPLIT:
                                act.wait_ge(w_used, n_e + w1b + 1)
                                if f > 1:
                                    act.wait_ge(e_g, k_e + f - 1)
                                act.activation(esil[:, f % 2, :], bank[2 * (f % 2)][:], ACT.Silu).then_inc(e_silu, 1)
                            if f and c == w1b + SPLIT:
                                transposed(k_e + f)
                        if c == PER_E:
                            transposed(k_e + FSTEPS)
                            if last:
                                before_root()
                            else:
                                gathered(e + 8 * r + 2)
                        if c == PER_E + 2:
                            act.wait_ge(w_used, n_e + PER_E)
                            act.wait_ge(y_add, 4 * e + 32 * r + 4)
                            for k in range(1 if last else 2):
                                ins = act.activation(y[:, 512 * k:512 * k + 512], bank[4 + k][:], ACT.Copy)
                            ins.then_inc(y_ev, 1)
                        if not (last and c >= PER_E):
                            n0 = first + c
                            if last:
                                split(n_e + c)
                            else:
                                at, times = slot(n0, r)
                                split_at(raw[:, at, :], w_raw[at], PER_E // RAW * 16 * e + 16 * times, n0, n_e + c - SPLIT + 1)

                with act.Fori(0, NE - 1) as e:
                    body(e, False)
                body(NE - 1, True)

            experts(0)
            act.wait_ge(count_ready, 1)
            most = act.value_load(cntu[0:1, 0:1])
            with act.If(most > SLOTS):
                experts(1)
            with act.Else():
                act.nop()

            for i in range(4):
                act.wait_ge(fo_done, i + 1)
                act.activation(fsq[:, i, :], bank[FINAL_BANK[i]][:], ACT.Square,
                               accum_out=small[:, i:i + 1]).then_inc(fo_sq, 1)
                if i % 2:
                    t = i // 2
                    act.wait_ge(fo_ms, t + 1)
                    act.activation(small[:, 6 + t:7 + t], small[:, 4 + t:5 + t], ACT.Sqrt, scale=1.0 / D,
                                   bias=small[:, 32:33]).then_inc(fo_rt, 1)

        @block.vector
        def _(dve):
            own = [0]

            def mine(ins):
                own[0] += 1
                ins.then_inc(dve_own, 1)

            def settled():
                dve.wait_ge(dve_own, own[0])

            def split_at(src, n, value, words=CW):
                dve.wait_ge(hi_ready, value)
                dve.tensor_tensor(wlo[:, n % SPLIT, 0:words], src[:, 0:words],
                                  whi[:, n % SPLIT, 0:words].bitcast(F32), ALU.subtract).then_inc(lo_ready, 1)

            def split(n):
                split_at(landed(n)[0], n, n + 1, used_words(n))

            def normalise(q, gain, parts):
                dve.wait_ge(rt_ready, q + 1)
                mine(dve.reciprocal(rstd[:], rstd[:]))
                if q == 0:
                    split(0)
                settled()
                for pair in range(5):
                    if pair < 4:
                        for c in (2 * pair, 2 * pair + 1):
                            ins = dve.scalar_tensor_tensor(hf[:, c, :], xT[:, c, :], par[:, 3, gain + c:gain + c + 1],
                                                           rstd[:], op0=ALU.mult, op1=ALU.mult)
                        ins.then_inc(hf_ready, 1)
                    if pair and parts:
                        dve.wait_ge(h_hi_s, 4 * q + pair)
                        pr = slice(2 * pair - 2, 2 * pair)
                        dve.tensor_tensor(h_hl[:, 1, pr, :], hf[:, pr, :], h_hl[:, 0, pr, :].bitcast(F32), ALU.subtract)\
                           .then_inc(h_lo_s, 1)

            dve.wait_ge(const, 5)
            mine(dve.tensor_scalar(ban[:, 0, :], dist, 0.0, NEG, ALU.is_lt, ALU.mult))
            mine(dve.tensor_scalar(ban[:, 1, :], dist, float(P), NEG, ALU.is_gt, ALU.mult))
            settled()
            mine(dve.tensor_tensor(mask[:, 0, :], ban[:, 0, :], ban[:, 1, :], ALU.add))
            for g, dilation in ((1, 4), (2, 16)):
                mine(dve.tensor_scalar(rest, dist, dilation - 1, None, ALU.bitwise_and))
                settled()
                mine(dve.tensor_scalar(ban[:, 1, :], rest, 0.0, NEG, ALU.is_gt, ALU.mult))
                settled()
                mine(dve.tensor_tensor(mask[:, g, :], ban[:, 0, :], ban[:, 1, :], ALU.add))
                settled()
            for i in range(4):
                dve.wait_ge(tr_done, 1 + i)
                dve.tensor_copy(xT[:, 2 * i:2 * i + 2, :], bank[1 + i][:].rearrange("p (a b) -> p a b", a=2))\
                   .then_inc(x_ready, 1)
            dve.wait_ge(par_ready, 1)
            normalise(0, G_MIX, True)
            split(1)
            split(2)

            def residual(n, lay, pair):
                xb = xT[:, 2 * pair:2 * pair + 2, :]
                dve.tensor_tensor(xb, bank[2 * (n % 2)][:].rearrange("p (a b) -> p a b", a=2), xb, ALU.add)\
                   .then_inc(x_ready, 1)

            taps = [0, 0]

            def conv_a_ops(lay, count):
                for _ in range(count):
                    k, c = divmod(taps[0] - KA * AB * lay, AB)
                    w = par[:, 1 + lay, 4 * k + c:4 * k + c + 1]
                    src = apad[:, c, k:k + S]
                    if k == 0:
                        ins = dve.tensor_scalar(aacc[:, c, :], src, w, par[:, 3, A_CB + 4 * lay + c:A_CB + 4 * lay + c + 1],
                                                ALU.mult, ALU.add)
                    else:
                        dve.wait_ge(conv_a, taps[0] - AB + 1)
                        ins = dve.scalar_tensor_tensor(aacc[:, c, :], src, w, aacc[:, c, :], op0=ALU.mult, op1=ALU.add)
                    ins.then_inc(conv_a, 1)
                    taps[0] += 1

            def conv_c_ops(lay, blocks):
                for k in range(KC):
                    for c in blocks:
                        at = C_CW + 12 * lay + 4 * k + c
                        w = par[:, 3, at:at + 1]
                        src = cpad[:, c, k:k + S]
                        if k == 0:
                            ins = dve.tensor_scalar(cacc[:, c, :], src, w, None, ALU.mult)
                        else:
                            dve.wait_ge(conv_c, taps[1] - len(blocks) + 1)
                            ins = dve.scalar_tensor_tensor(cacc[:, c, :], src, w, cacc[:, c, :], op0=ALU.mult, op1=ALU.add)
                        ins.then_inc(conv_c, 1)
                        taps[1] += 1

            def head_mask(lay, h):
                k = 4 * lay + h
                dve.wait_ge(sc_done, k + 1)
                mine(dve.scalar_tensor_tensor(prob0, bank[4][:, 0:384].rearrange("p (a b) -> p a b", a=3), 0.125,
                                              mask[:, :, P:S], op0=ALU.mult, op1=ALU.add))
                mine(dve.scalar_tensor_tensor(prob1[:, 0:2, :], bank[5][:].rearrange("p (a b) -> p a b", a=2), 0.125,
                                              mask[:, 0:2, :], op0=ALU.mult, op1=ALU.add))
                mine(dve.scalar_tensor_tensor(prob1[:, 2, :], bank[6][:, 0:256], 0.125, mask[:, 2, :],
                                              op0=ALU.mult, op1=ALU.add))
                settled()
                mine(dve.tensor_reduce(small[:, 2:3], prob0.rearrange("p a b -> p (a b)"), AX.X, ALU.max))
                mine(dve.tensor_reduce(small[:, 3:4], prob1.rearrange("p a b -> p (a b)"), AX.X, ALU.max))
                settled()
                dve.tensor_scalar(small[:, 0:2], small[:, 2:4], -1.0, None, ALU.mult).then_inc(mx_ready, 1)

            def head_out(lay, h):
                k = 4 * lay + h
                dve.wait_ge(pv_done, k + 1)
                mine(dve.reciprocal(small[:, 6:8], small[:, 4:6]))
                settled()
                dve.tensor_scalar(otok[:, 0, DH * h:DH * h + DH], bank[7][:, 0:64], small[:, 6:7], None, ALU.mult)
                dve.tensor_scalar(otok[:, 1, DH * h:DH * h + DH], bank[7][:, 64:128], small[:, 7:8], None, ALU.mult)\
                   .then_inc(o_ready, 1)

            def post(n):
                lay, c = local(n)
                b = BASE[lay]
                what, i = PLAN[c]
                src = bank[2 * (n % 2)]
                dve.wait_ge(w_used, n + 1)
                if what in ("aval", "ch"):
                    s_, val = taken(n - 1)
                    dve.wait_ge(s_, val)
                    dve.wait_ge(pads, 2 * (lay + 1))
                    for k in range(2):
                        at = 2 * i + k
                        dst = apad[:, at, KA - 1:] if what == "aval" else cpad[:, at, KC - 1:]
                        gate = (agate if what == "aval" else ccv)[:, at, :]
                        col = 62 * lay + 2 * (IN_BLOCK[what] + i) + k
                        ins = dve.scalar_tensor_tensor(dst, src[:, 256 * k:256 * k + 256], par[:, 0, col:col + 1], gate,
                                                       op0=ALU.add, op1=ALU.mult)
                    ins.then_inc(out_dve, 1)
                elif what == "v":
                    dve.wait_ge(in_vb, 16 * (lay + 1))
                    dve.tensor_tensor(vtok[:, :, 256 * i:256 * i + 256], src[:].rearrange("p (a b) -> p a b", a=2),
                                      vbias[:, 256 * i:256 * i + 256].unsqueeze(1).to_broadcast([P, TB, 256]), ALU.add)\
                       .then_inc(out_dve, 1)
                elif what in ("wo", "xo"):
                    residual(n, lay, i)
                if n == 2:
                    dve.wait_ge(mrt_ready, 1)
                    mine(dve.reciprocal(rstd[:], rstd[:]))
                    settled()
                    mine(dve.tensor_tensor(memhat[:], memhat[:], rstd[:].unsqueeze(1).to_broadcast([P, DB, S]), ALU.mult))
                if c in (AT["aval", 1], AT["ch", 0] + 1, AT["ch", 1] + 1):
                    s_, val = taken(b + AT["aval", 1] if c < 10 else b + AT["ch", 0] if c < 18 else b + AT["ch", 1])
                    dve.wait_ge(s_, val)
                for h in range(HEADS):
                    if c == HEAD_AT[h] + 3:
                        head_out(lay, h)
                for h in range(HEADS):
                    if c == HEAD_AT[h]:
                        head_mask(lay, h)
                if c in CONV_C_AT:
                    conv_c_ops(lay, CONV_C_AT[c])
                if c == C_AT:
                    dve.wait_ge(conv_c, taps[1])
                    s_, val = taken(b + AT["cb", 1])
                    dve.wait_ge(s_, val)
                    dve.tensor_tensor(cacc, cacc, cb, ALU.mult).then_inc(c_f, 1)
                if c in CONV_A_AT:
                    conv_a_ops(lay, CONV_A_AT[c])
                if c == C_AT:
                    dve.wait_ge(c_hi_s, lay + 1)
                    dve.tensor_tensor(c_lo, cacc, c_hi.bitcast(F32), ALU.subtract).then_inc(c_lo_s, 1)
                if c == LN_AT[0]:
                    dve.wait_ge(ln_st, 2 * lay + 1)
                    dve.scalar_tensor_tensor(aacc, bank[ln_bank(b + LN_AT[0] + 1)][:, 0:256].unsqueeze(1).to_broadcast([P, AB, S]),
                                             -float(D) / AW, aacc, op0=ALU.mult, op1=ALU.add).then_inc(ln_xc, 1)
                if c == LN_AT[1]:
                    dve.wait_ge(ln_rt, lay + 1)
                    mine(dve.reciprocal(rstd[:], rstd[:]))
                    settled()
                    dve.tensor_tensor(aacc, aacc, rstd[:].unsqueeze(1).to_broadcast([P, AB, S]), ALU.mult).then_inc(ln_y, 1)
                    dve.wait_ge(a_hi_s, lay + 1)
                    dve.tensor_tensor(a_lo, asq, a_hi.bitcast(F32), ALU.subtract).then_inc(a_lo_s, 1)
                if c == OT_AT:
                    dve.wait_ge(o_hi_s, lay + 1)
                    dve.tensor_tensor(o_lo, bank[4][:].rearrange("p (a b) -> p a b", a=2), o_hi.bitcast(F32),
                                      ALU.subtract).then_inc(o_lo_s, 1)
                if c == MEM_AT[0]:
                    settled()
                    for half in range(2):
                        for k in range(4 * half, 4 * half + 4):
                            at = G_MEM + 8 * lay + k
                            ins = dve.tensor_scalar(hf[:, k, :], memhat[:, k, :], par[:, 3, at:at + 1], None, ALU.mult)
                        ins.then_inc(mf_ready, 1)
                if c == MEM_AT[1]:
                    for half in range(2):
                        dve.wait_ge(m_hi_s, 2 * lay + half + 1)
                        dve.tensor_tensor(m_lo[:, 4 * half:4 * half + 4, :], hf[:, 4 * half:4 * half + 4, :],
                                          m_hi[:, 4 * half:4 * half + 4, :].bitcast(F32), ALU.subtract).then_inc(m_lo_s, 1)
                if c == AT["ga", 3]:
                    for pair in range(4):
                        pr = slice(2 * pair, 2 * pair + 2)
                        dve.wait_ge(mg_hi_s, 4 * lay + pair + 1)
                        dve.tensor_tensor(h_hl[:, 1, pr, :], merged[:, pr, :], h_hl[:, 0, pr, :].bitcast(F32), ALU.subtract)\
                           .then_inc(mg_lo_s, 1)
                if c == AT["wo", 3] + 1:
                    dve.wait_ge(m_lo_s, 2 * lay + 2)
                    normalise(3 * lay + 1, G_X + 8 * lay, True)
                if c == AT["xv", 0]:
                    for i in range(4):
                        dve.wait_ge(xs_done, 4 * lay + i + 1)
                        mine(dve.tensor_reduce(small[:, 24 + 2 * i:26 + 2 * i],
                                               bank[4 + i][:].rearrange("p (a b) -> p a b", a=2), AX.X, ALU.max))
                        settled()
                        dve.tensor_scalar(small[:, 8 + 2 * i:10 + 2 * i], small[:, 24 + 2 * i:26 + 2 * i], -1.0 / 16, None,
                                          ALU.mult).then_inc(xm_ready, 2)
                    for i in range(4):
                        dve.wait_ge(xp_ready, 8 * lay + 2 * i + 2)
                        mine(dve.reciprocal(small[:, 16 + 2 * i:18 + 2 * i], small[:, 16 + 2 * i:18 + 2 * i]))
                        settled()
                        for k in range(2):
                            ins = dve.tensor_scalar(probx[:, 2 * i + k, :], probx[:, 2 * i + k, :],
                                                    small[:, 16 + 2 * i + k:17 + 2 * i + k], None, ALU.mult)
                        ins.then_inc(xn_ready, 1)
                if c == AT["xv", 3]:
                    for i in range(4):
                        dve.wait_ge(xo_hi_s, 4 * lay + i + 1)
                        dve.tensor_tensor(h_hl[:, 1, 2 * i:2 * i + 2, :], bank[4 + i][:].rearrange("p (a b) -> p a b", a=2),
                                          h_hl[:, 0, 2 * i:2 * i + 2, :].bitcast(F32), ALU.subtract).then_inc(xo_lo_s, 1)
                if c == AT["xo", 3]:
                    if lay == 0:
                        dve.memset(zerosf, 0.0).then_inc(z_ready, 1)
                    normalise(3 * lay + 2, G_FFN + 8 * lay, lay == 0)

            def ffn_dve(i, j):
                dve.wait_ge(silu_s, i + 1)
                dve.tensor_tensor(gf[:, j, :], bank[2 * j + 1][:], sil[:, j, :], ALU.mult).then_inc(g_s, 1)
                dve.wait_ge(g_hi_s, i + 1)
                dve.tensor_tensor(g_lo[:, j, :], gf[:, j, :], g_hi[:, j, :].bitcast(F32), ALU.subtract).then_inc(g_lo_s, 1)

            for lay in range(LAYERS):
                b = BASE[lay]
                for n in range(b + SPLIT, b + C_FFN):
                    post(n - SPLIT)
                    split(n)
                if lay == 0:
                    f = b + C_FFN
                    for k in range(3):
                        post(f - 3 + k)
                        if k < 2:
                            split(f + k)
                    with dve.Fori(0, (FFB - 1) // 2) as i:
                        for c in range(6):
                            n0 = f + 2 + c
                            if c == 2:
                                ffn_dve(2 * i, 0)
                            if c == 4:
                                ffn_dve(2 * i + 1, 1)
                            split_at(raw[:, n0 % RAW, :], n0, 6 * i + n0 + 1)
                    split(f + 3 * FFB - 1)
                    ffn_dve(FFB - 1, 0)
                    split(BASE[1])
                    split(BASE[1] + 1)
                    for i in range(4):
                        dve.wait_ge(w_used, BASE[1])
                        xb = xT[:, 2 * i:2 * i + 2, :]
                        dve.tensor_tensor(xb, bank[4 + i][:].rearrange("p (a b) -> p a b", a=2), xb, ALU.add)\
                           .then_inc(x_ready, 1)
                    normalise(3, G_MIX + 8, True)
                    split(BASE[1] + 2)
                else:
                    for n in range(MOE - SPLIT, MOE):
                        post(n)
                        split(n + SPLIT)

            dve.wait_ge(rl_done, 1)
            dve.tensor_copy(lgT, bank[7][0:NE, 256:512]).then_inc(lt_ready, 1)
            dve.wait_ge(lt_done, 1)
            mine(dve.tensor_copy(lg, bank[7][:, 256:272].rearrange("p (b e) -> p b e", e=NE)))
            settled()
            for b in range(TB):
                mine(dve.max(top[:, b, :], lg[:, b, :]))
            settled()
            for b in range(TB):
                mine(dve.max_index(idxu[:, b, :], top[:, b, :], lg[:, b, :]))
                mine(dve.tensor_tensor(wts[:, b:b + 1], top[:, b, 1:2], top[:, b, 0:1], ALU.subtract))
            settled()
            dve.tensor_copy(idxf, idxu[:]).then_inc(rl_ready, 1)
            dve.wait_ge(rl_ready, 1)
            dve.wait_ge(rt_const, 4)
            for b in range(TB):
                mine(dve.tensor_scalar(oh0[:, b, :], iota8, idxf[:, b, 0:1], None, ALU.is_equal))
                mine(dve.tensor_scalar(oh1[:, b, :], iota8, idxf[:, b, 1:2], None, ALU.is_equal))
            settled()
            dve.tensor_tensor(msk, oh0, oh1, ALU.add).then_inc(mk_ready, 1)
            dve.wait_ge(cnt_done, 1)
            mine(dve.tensor_scalar(posm, bank[7][:, 288:304].rearrange("p (b e) -> p b e", e=NE), 1.0, None, ALU.add))
            mine(dve.tensor_reduce(cntf, bank[7][:, 304:312], AX.X, ALU.max))
            dve.wait_ge(mk_ready, 1)
            settled()
            mine(dve.tensor_tensor(posm, posm, msk, ALU.mult))
            dve.tensor_copy(cntu[:], cntf).then_inc(count_ready, 1)

            def weights():
                dve.wait_ge(re_ready, 1)
                mine(dve.tensor_scalar(wts[:, 4:6], wts[:, 2:4], 1.0, None, ALU.add))
                settled()
                mine(dve.reciprocal(wts[:, 6:8], wts[:, 4:6]))
                settled()
                mine(dve.tensor_tensor(wts[:, 8:10], wts[:, 2:4], wts[:, 6:8], ALU.mult))
                for b in range(TB):
                    mine(dve.tensor_scalar(comb[:, b, :], oh0[:, b, :], wts[:, 6 + b:7 + b], None, ALU.mult))
                settled()
                for b in range(TB):
                    mine(dve.scalar_tensor_tensor(comb[:, b, :], oh1[:, b, :], wts[:, 8 + b:9 + b], comb[:, b, :],
                                                  op0=ALU.mult, op1=ALU.add))
                settled()

            def experts(r):
                first = MOE + NE * PER_E * r
                dve.tensor_scalar(posr, posm, -1.0 - SLOTS * r, None, ALU.add).then_inc(round_own, 1)
                dve.wait_ge(round_own, 2 * r + 1)
                for b in range(TB):
                    ins = dve.tensor_scalar(sel[:, b, 0, :], iota, posr[:, b, 0:1], None, ALU.is_equal)
                ins.then_inc(sel0_ready, 1)
                if r == 0:
                    weights()
                for b in range(TB):
                    ins = dve.tensor_tensor(sel[:, b, 1:NE, :], iota.unsqueeze(1).to_broadcast([P, NE - 1, SLOTS]),
                                            posr[:, b, 1:NE].unsqueeze(2).to_broadcast([P, NE - 1, SLOTS]), ALU.is_equal)
                ins.then_inc(round_own, 1)
                dve.wait_ge(sel0_ready, r + 1)
                dve.wait_ge(round_own, 2 * r + 2)
                for b in range(TB):
                    ins = dve.tensor_tensor(wsel[:, b, :, :], sel[:, b, 0:NE, :],
                                            comb[:, b, :].unsqueeze(2).to_broadcast([P, NE, SLOTS]), ALU.mult)
                ins.then_inc(sel_ready, 1)

                def gathered(count):
                    dve.wait_ge(he_hi_s, count)
                    for k in range(2):
                        ins = dve.tensor_tensor(he_lo[:, 512 * k:512 * k + 512], bank[2 + k][:],
                                                he_hi[:, 512 * k:512 * k + 512].bitcast(F32), ALU.subtract)
                    ins.then_inc(he_lo_s, 1)

                def transposed(count):
                    dve.wait_ge(e_hi, count)
                    dve.tensor_tensor(eT_lo, bank[6][:], eT_hi.bitcast(F32), ALU.subtract).then_inc(e_lo, 1)

                def scattered(count, q):
                    dve.wait_ge(y_sc, count)
                    xb = xT[:, 2 * q:2 * q + 2, :]
                    dve.tensor_tensor(xb, bank[7][:].rearrange("p (a b) -> p a b", a=2), xb, ALU.add).then_inc(y_add, 1)

                if r:
                    for c in range(SPLIT):
                        split(first + c)
                gathered(8 * r + 1)

                def body(e, last):
                    k_e = FSTEPS * e + NE * FSTEPS * r
                    for c in range(SPLIT, PER_E + SPLIT):
                        for f in range(FSTEPS):
                            w1b = 1 if f == 0 else 6 * f - 1
                            w3b = w1b + 2
                            if f and c == w1b + SPLIT:
                                transposed(k_e + f)
                            if c == w3b + SPLIT:
                                dve.wait_ge(e_silu, k_e + f + 1)
                                dve.wait_ge(w_used, PER_E * e + first + w3b + 1)
                                dve.tensor_tensor(eg, bank[2 * (f % 2) + 1][:], esil[:, f % 2, :], ALU.mult).then_inc(e_g, 1)
                            if f < 4 and c == w3b + SPLIT + 1:
                                scattered(4 * e + 32 * r + f + 1, f)
                        if c == PER_E:
                            transposed(k_e + FSTEPS)
                            if not last:
                                gathered(e + 8 * r + 2)
                        if last and c == PER_E + 2:
                            dve.wait_ge(w_used, PER_E * e + first + PER_E)
                            dve.wait_ge(y_add, 32 * (r + 1))
                            dve.tensor_copy(y[:, 512:D], bank[5][:]).then_inc(y_half, 1)
                        if not (last and c >= PER_E):
                            n0 = first + c
                            if last:
                                split(first + PER_E * e + c)
                            else:
                                split_at(raw[:, slot(n0, r)[0], :], n0, PER_E * e + n0 + 1)

                with dve.Fori(0, NE - 1) as e:
                    body(e, False)
                body(NE - 1, True)

            settled()
            experts(0)
            most = dve.value_load(cntu[0:1, 0:1])
            with dve.If(most > SLOTS):
                experts(1)
            with dve.Else():
                dve.nop()
            dve.wait_ge(in_fin, 16)
            for t in range(TB):
                dve.wait_ge(fo_sq, 2 * t + 2)
                dve.tensor_tensor(small[:, 4 + t:5 + t], small[:, 2 * t:2 * t + 1], small[:, 2 * t + 1:2 * t + 2], ALU.add)\
                   .then_inc(fo_ms, 1)
                dve.wait_ge(fo_rt, t + 1)
                mine(dve.reciprocal(small[:, 6 + t:7 + t], small[:, 6 + t:7 + t]))
                settled()
                for i in range(2):
                    dve.scalar_tensor_tensor(yout[:, t, 512 * i:512 * i + 512], bank[FINAL_BANK[2 * t + i]][:],
                                             small[:, 6 + t:7 + t], gfin[:, 512 * i:512 * i + 512],
                                             op0=ALU.mult, op1=ALU.mult).then_inc(fo_ready, 1)

        @block.tensor
        def _(pe):
            def three(o, st, mv, start, stop, **kw):
                pe.matmul(o, st[0], mv[0], start=start, stop=False, **kw)
                pe.matmul(o, st[0], mv[1], start=False, stop=False, **kw)
                return pe.matmul(o, st[1], mv[0], start=False, stop=stop, **kw)

            def wt(n, k, cols, at, width):
                return tuple(w[:, n % SPLIT, k * cols + at:k * cols + at + width] for w in (whi, wlo))

            def parts(hi, lo, k):
                return hi[:, k, :], lo[:, k, :]

            h_hi, h_lo = h_hl[:, 0, :, :], h_hl[:, 1, :, :]

            def free(n):
                lay, c = local(n)
                if c >= 2:
                    s_, val = taken(n - 2)
                    pe.wait_ge(s_, val)

            def chunk_in(n, parts_ready=None):
                pe.wait_ge(lo_ready, n + 1)
                free(n)
                for o in range(2):
                    for k in range(DB):
                        if parts_ready and o == 0 and k % 2 == 0:
                            pe.wait_ge(parts_ready[0], parts_ready[1] + k // 2 + 1)
                        ins = three(bank[2 * (n % 2)][:, 256 * o:256 * o + 256], wt(n, k, 256, 128 * o, 128),
                                    parts(h_hi, h_lo, k), k == 0, k == DB - 1)
                ins.then_inc(w_used, 1)

            def chunk_tok(n, hi, lo):
                pe.wait_ge(lo_ready, n + 1)
                free(n)
                for t in range(TB):
                    for k in range(DB):
                        tok = tuple(a[:, k, P * t:P * t + P] for a in (hi, lo))
                        ins = three(bank[2 * (n % 2)][:, 256 * t:256 * t + 256], tok, wt(n, k, 256, 0, 256),
                                    k == 0, k == DB - 1)
                ins.then_inc(w_used, 1)

            def chunk_mem(n):
                pe.wait_ge(lo_ready, n + 1)
                free(n)
                for o in range(2):
                    for k in range(DB):
                        ins = three(bank[2 * (n % 2)][:, 256 * o:256 * o + 256], wt(n, k, 256, 128 * o, 128),
                                    parts(m_hi, m_lo, k), k == 0, k == DB - 1)
                ins.then_inc(w_used, 1)

            def chunk_out(n, hi, lo, kb):
                pe.wait_ge(lo_ready, n + 1)
                free(n)
                for o in range(4):
                    for k in range(kb):
                        ins = three(bank[2 * (n % 2) + o // 2][:, 256 * (o % 2):256 * (o % 2) + 256],
                                    wt(n, k, 512, 128 * o, 128), parts(hi, lo, k), k == 0, k == kb - 1)
                ins.then_inc(w_used, 1)

            def stat(src, nb, to=7):
                for k in range(nb):
                    ins = pe.matmul(bank[to][:, 0:256], ones[:], src[:, k, :], start=k == 0, stop=k == nb - 1)
                return ins

            def norm_pair(q, pair):
                if q in SUMMED and pair < 3:
                    if pair == 2:
                        pe.wait_ge(sq_sum, 5 * SUMMED.index(q) + 5)
                        pe.matmul(norm_bank(q)[:, 0:256], ones[:], sq[:, 0, :], start=True, stop=False)
                    return
                pe.wait_ge(sq_ready, 4 * q + pair + 1)
                for k in (2 * pair, 2 * pair + 1):
                    ins = pe.matmul(norm_bank(q)[:, 0:256], ones[:], sq[:, k, :], start=k == 0, stop=k == DB - 1)
                if pair == 3:
                    ins.then_inc(ss_done, 1)

            def turn_in(src, banks):
                for i in range(4):
                    for k in range(4):
                        c, t = 2 * i + k // 2, k % 2
                        ins = pe.transpose(bank[banks[i]][:, P * k:P * k + P], src[:, t, P * c:P * c + P], ident[:])
                    ins.then_inc(tr_done, 1)

            pe.wait_ge(const, 5)
            pe.wait_ge(in_x, 32)
            turn_in(xin, (1, 2, 3, 4))
            pe.wait_ge(in_par, 11 * 16)
            for t in range(4):
                rows = 112 if t == 3 else 124
                ins = pe.transpose(bank[0][:, P * t:P * t + rows], prow[0:rows, t, :], ident[0:rows, 0:rows])
            ins.then_inc(tr_done, 1)
            for pair in range(4):
                norm_pair(0, pair)

            def scores(lay, h):
                if h == 0:
                    s_, val = taken(BASE[lay] + AT["k", 2])
                    pe.wait_ge(s_, val)
                for g in range(GROUPS):
                    c, p0 = 2 * g + h // 2, 64 * (h % 2)
                    q_, k_ = qT[p0:p0 + 64, c, :], kT[p0:p0 + 64, c, :]
                    pe.matmul(bank[4][:, P * g:P * g + P], q_[:, 0:P], k_[:, 0:P], start=True, stop=True)
                    o = bank[5][:, 256 * g:256 * g + 256] if g < 2 else bank[6][:, 0:256]
                    ins = pe.matmul(o, q_[:, P:S], k_, start=True, stop=True)
                ins.then_inc(sc_done, 1)

            def values(lay, h):
                k = 4 * lay + h
                pe.wait_ge(pr_ready, k + 1)
                for g in range(GROUPS):
                    pe.transpose(bank[4][:, P * g:P * g + P], prob0[:, g, :], ident[:])
                    for t in range(TB):
                        o = bank[5][:, 256 * g + P * t:256 * g + P * t + P] if g < 2 else bank[6][:, P * t:P * t + P]
                        ins = pe.transpose(o, prob1[:, g, P * t:P * t + P], ident[:])
                ins.then_inc(pt_done, 1)

            def weigh(lay, h):
                k = 4 * lay + h
                pe.wait_ge(pT_ready, k + 1)
                if h == 0:
                    s_, val = taken(BASE[lay] + AT["v", 2])
                    pe.wait_ge(s_, val)
                for g in range(GROUPS):
                    at = 256 * g + DH * h
                    pe.matmul(bank[7][:, 0:64], pT0[:, g, :], vtok[:, 0, at:at + DH], start=g == 0, stop=g == GROUPS - 1)
                for g in range(GROUPS):
                    at = 256 * g + DH * h
                    for t in range(TB):
                        ins = pe.matmul(bank[7][:, 64:128], pT1[:, g, P * t:P * t + P], vtok[:, t, at:at + DH],
                                        start=g == 0 and t == 0, stop=g == GROUPS - 1 and t == TB - 1)
                ins.then_inc(pv_done, 1)

            for lay in range(LAYERS):
                b = BASE[lay]
                for c, (what, i) in enumerate(PLAN):
                    n = b + c
                    if n == 1:
                        pe.wait_ge(in_mem, 16)
                        turn_in(min_, (4, 5, 6, 7))
                    if n == 3:
                        pe.wait_ge(msq_sum, 4)
                        stat(msq[:, 0:DB:2, :], DB // 2).then_inc(mss_done, 1)
                    if c == LN_AT[0] + 1:
                        pe.wait_ge(conv_a, KA * AB * (lay + 1))
                        stat(aacc, AB, ln_bank(n)).then_inc(ln_st, 1)
                    if c == LN_AT[1] + 1:
                        pe.wait_ge(ln_sq, lay + 1)
                        stat(asq, AB, ln_bank(n)).then_inc(ln_st, 1)
                    for h in range(HEADS):
                        if c == HEAD_AT[h] + 3:
                            values(lay, h)
                        if c == HEAD_AT[h] + 4:
                            weigh(lay, h)
                    for h in range(HEADS):
                        if c == HEAD_AT[h] + 1:
                            scores(lay, h)
                    if c == OT_AT + 1:
                        pe.wait_ge(o_ready, 4 * lay + 4)
                        for i in range(2):
                            for t in range(TB):
                                ins = pe.transpose(bank[4][:, 256 * i + P * t:256 * i + P * t + P],
                                                   otok[:, t, P * i:P * i + P], ident[:])
                        ins.then_inc(oT_done, 1)
                    for pair in range(4):
                        if c == AT["wo", pair] + 2:
                            norm_pair(3 * lay + 1, pair)
                        if c == AT["xo", pair] + 2:
                            norm_pair(3 * lay + 2, pair)
                    if c == AT["xv", 1]:
                        for cc in (AT["xk", 3], AT["xq", 3]):
                            s_, val = taken(b + cc)
                            pe.wait_ge(s_, val)
                        for hh in range(XH):
                            for t in range(TB):
                                for k in range(2):
                                    ins = pe.matmul(bank[4 + hh][:, 256 * t:256 * t + 256],
                                                    qx[:, 2 * hh + k, P * t:P * t + P], kx[:, 2 * hh + k, :],
                                                    start=k == 0, stop=k == 1)
                            ins.then_inc(xs_done, 1)
                    if c == AT["xv", 3]:
                        for hh in range(XH):
                            pe.wait_ge(xn_ready, 4 * lay + hh + 1)
                            for m in range(TB):
                                for t in range(TB):
                                    ins = pe.transpose(bank[4 + hh][:, 256 * m + P * t:256 * m + P * t + P],
                                                       probx[:, 2 * hh + t, P * m:P * m + P], ident[:])
                            ins.then_inc(xpt_done, 1)
                    if c == AT["xo", 0]:
                        s_, val = taken(b + AT["xv", 3])
                        pe.wait_ge(s_, val)
                        for hh in range(XH):
                            pe.wait_ge(xpT_ready, 4 * lay + hh + 1)
                            for o in range(2):
                                for m in range(TB):
                                    at = 256 * hh + P * o
                                    ins = pe.matmul(bank[4 + hh][:, 256 * o:256 * o + 256], vx[:, m, at:at + P],
                                                    pTx[:, 2 * hh + m, :], start=m == 0, stop=m == TB - 1)
                            ins.then_inc(xpv_done, 1)
                    if what == "v":
                        chunk_tok(n, h_hi, h_lo)
                    elif what == "xv":
                        chunk_tok(n, m_hi, m_lo)
                    elif what == "xk":
                        if i == 0:
                            pe.wait_ge(m_lo_s, 2 * lay + 2)
                        chunk_mem(n)
                    elif what == "cout":
                        pe.wait_ge(c_lo_s, lay + 1)
                        chunk_out(n, c_hi, c_lo, AB)
                    elif what == "aout":
                        pe.wait_ge(a_lo_s, lay + 1)
                        chunk_out(n, a_hi, a_lo, AB)
                    elif what == "bout":
                        pe.wait_ge(o_lo_s, lay + 1)
                        chunk_out(n, o_hi, o_lo, 2)
                    elif c == 0:
                        chunk_in(n, (h_lo_s, 12 * lay))
                    elif (what, i) == ("wo", 0):
                        chunk_in(n, (mg_lo_s, 4 * lay))
                    elif (what, i) == ("xq", 0):
                        chunk_in(n, (h_lo_s, 12 * lay + 4))
                    elif (what, i) == ("xo", 0):
                        chunk_in(n, (xo_lo_s, 4 * lay))
                    else:
                        chunk_in(n)
                for pair in (2, 3):
                    norm_pair(3 * lay + 2, pair)
                if lay == 0:
                    f = b + C_FFN

                    def up(n0, value, bk, new=False):
                        pe.wait_ge(lo_ready, value)
                        for o in range(2):
                            for k in range(DB):
                                if new and o == 0 and k % 2 == 0:
                                    pe.wait_ge(h_lo_s, 8 + k // 2 + 1)
                                ins = three(bank[bk][:, 256 * o:256 * o + 256], wt(n0, k, 256, 128 * o, 128),
                                            parts(h_hi, h_lo, k), k == 0, k == DB - 1)
                        ins.then_inc(w_used, 1)

                    def down(n0, value, steps, j):
                        pe.wait_ge(lo_ready, value)
                        pe.wait_ge(g_lo_s, steps)
                        for o in range(DB):
                            for k in range(2):
                                hid = tuple(a[:, j, 256 * k:256 * k + 256] for a in (g_hi, g_lo))
                                ins = three(bank[4 + o // 2][:, 256 * (o % 2):256 * (o % 2) + 256],
                                            wt(n0, k, D, P * o, P), hid, False, False,
                                            skip_group_check=True)
                        ins.then_inc(w_used, 1)

                    up(f, f + 1, 0, True)
                    up(f + 1, f + 2, 1)
                    pe.wait_ge(z_ready, 1)
                    for o in range(4):
                        pe.matmul(bank[4 + o][:], zeros[:, 0:P], zeros, start=True, stop=False, skip_group_check=True)
                    with pe.Fori(0, (FFB - 1) // 2) as i:
                        for j in (1, 2):
                            c = 3 * (j - 1)
                            bk = 2 * (j % 2)
                            up(f + 2 + c, 6 * i + f + 3 + c, bk)
                            up(f + 3 + c, 6 * i + f + 4 + c, bk + 1)
                            down(f + 4 + c, 6 * i + f + 5 + c, 2 * i + j, (j - 1) % 2)
                    down(f + 3 * FFB - 1, f + 3 * FFB, FFB, (FFB - 1) % 2)
                    for pair in range(4):
                        norm_pair(3, pair)

            def rows(i):
                for k in range(4):
                    c = 4 * (i % 2) + k
                    ins = pe.transpose(bank[i][:, P * k:P * k + P], hf[:, c, P * (i // 2):P * (i // 2) + P], ident[:])
                ins.then_inc(ht_done, 1)

            pe.wait_ge(in_rt, 16)
            for k in range(DB):
                if k % 2 == 0:
                    pe.wait_ge(hf_ready, 20 + k // 2 + 1)
                ins = pe.matmul(bank[7][0:NE, 256:512], router[:, k, :], hf[:, k, :], start=k == 0, stop=k == DB - 1)
            ins.then_inc(rl_done, 1)
            pe.wait_ge(lt_ready, 1)
            for t in range(TB):
                ins = pe.transpose(bank[7][:, 256 + NE * t:256 + NE * t + NE], lgT[:, P * t:P * t + P], ident[0:NE, 0:NE])
            ins.then_inc(lt_done, 1)
            for i in range(2):
                rows(i)
            pe.wait_ge(mk_ready, 1)
            pe.wait_ge(rt_const, 4)
            pe.matmul(bank[7][:, 288:296], strict, msk[:, 0, :], start=True, stop=True)
            pe.matmul(bank[7][:, 296:304], allone, msk[:, 0, :], start=True, stop=False)
            pe.matmul(bank[7][:, 296:304], strict, msk[:, 1, :], start=False, stop=True)
            pe.matmul(bank[7][:, 304:312], allone, msk[:, 0, :], start=True, stop=False)
            pe.matmul(bank[7][:, 304:312], allone, msk[:, 1, :], start=False, stop=True).then_inc(cnt_done, 1)
            for i in range(2, 4):
                rows(i)

            def experts(r):
                first = MOE + NE * PER_E * r
                pe.wait_ge(sel0_ready, r + 1)
                if r == 0:
                    pe.wait_ge(ht_ready, 4)

                def gather(e):
                    for c in range(DB):
                        for t in range(TB):
                            ins = pe.matmul(bank[2 + c // 4][:, P * (c % 4):P * (c % 4) + P], htok[:, t, P * c:P * c + P],
                                            sel[:, t, bass.ds(e, 1), :].rearrange("p a b -> p (a b)"),
                                            start=t == 0, stop=t == TB - 1)
                    ins.then_inc(ga_done, 1)

                def up(c, e, o):
                    n0 = first + c
                    half = c % 2
                    pe.wait_ge(lo_ready, PER_E * e + n0 + 1)
                    for k in range(4):
                        tok = tuple(a[:, P * (4 * half + k):P * (4 * half + k) + P] for a in (he_hi, he_lo))
                        ins = three(o, tok, wt(n0, k, 512, 0, 512), half == 0 and k == 0, half == 1 and k == 3)
                    ins.then_inc(w_used, 1)

                def turn(f, k_e):
                    pe.wait_ge(e_g, k_e + f + 1)
                    for k in range(4):
                        ins = pe.transpose(bank[6][:, P * k:P * k + P], eg[:, P * k:P * k + P], ident[:])
                    ins.then_inc(e_tr, 1)

                def down(c, e, f, half, k_e):
                    n0 = first + c
                    pe.wait_ge(lo_ready, PER_E * e + n0 + 1)
                    if half == 0:
                        pe.wait_ge(e_lo, k_e + f + 1)
                    for k in range(2):
                        at = P * (2 * half + k)
                        hid = (eT_hi[:, at:at + P], eT_lo[:, at:at + P])
                        for o in range(2):
                            ins = three(bank[4 + o][:], hid, wt(n0, k, D, 512 * o, 512), f == 0 and half == 0 and k == 0,
                                        f == FSTEPS - 1 and half == 1 and k == 1)
                    ins.then_inc(w_used, 1)

                def scatter(e, q):
                    for o in range(2):
                        c = 2 * q + o
                        ins = pe.matmul(bank[7][:, 256 * o:256 * o + 256], y[:, P * c:P * c + P],
                                        wselT[:, bass.ds(e, 1), :].rearrange("p a b -> p (a b)"), start=True, stop=True)
                    ins.then_inc(y_sc, 1)

                gather(0)
                pe.wait_ge(rt_const, 5)
                pe.wait_ge(sel_ready, r + 1)
                for i in range(4):
                    for k in range(4):
                        e, t = 2 * i + k // 2, k % 2
                        ins = pe.transpose(bank[WT_BANK[i]][:, P * k:P * k + P], wsel[:, t, e, :], ident[:])
                    ins.then_inc(wt_done, 1)
                pe.wait_ge(wt_ready, 4 * r + 2)
                def final_rows(i):
                    for k in range(4):
                        c = 4 * (i % 2) + k
                        pe.matmul(bank[FINAL_BANK[i]][:, P * k:P * k + P], xT[:, c, P * (i // 2):P * (i // 2) + P],
                                  ident[:], start=k == 0, stop=False, skip_group_check=True)

                def body(e, last):
                    k_e = FSTEPS * e + NE * FSTEPS * r
                    pe.wait_ge(he_lo_s, e + 8 * r + 1)
                    c = 0
                    for f in range(FSTEPS + 1):
                        bk = 2 * (f % 2)
                        if f < FSTEPS:
                            if f > 1:
                                pe.wait_ge(e_g, k_e + f - 1)
                            up(c, e, bank[bk][:])
                            up(c + 1, e, bank[bk][:])
                            c += 2
                        if f:
                            turn(f - 1, k_e)
                        if last and f == FSTEPS - 2:
                            pe.wait_ge(y_add, 32 * (r + 1))
                            final_rows(2)
                        if last and f == FSTEPS - 1:
                            for i in range(2):
                                final_rows(i)
                        if f == FSTEPS:
                            if last:
                                final_rows(3)
                            else:
                                gather(e + 1)
                        if f < FSTEPS:
                            up(c, e, bank[bk + 1][:])
                            up(c + 1, e, bank[bk + 1][:])
                            c += 2
                        if f < 4:
                            if f == 0:
                                pe.wait_ge(y_ev, e + 8 * r + 1)
                            else:
                                pe.wait_ge(y_add, 4 * e + 32 * r + f)
                            scatter(e, f)
                        if f:
                            down(c, e, f - 1, 0, k_e)
                            down(c + 1, e, f - 1, 1, k_e)
                            c += 2

                with pe.Fori(0, NE - 1) as e:
                    body(e, False)
                body(NE - 1, True)
                pe.wait_ge(y_ev, NE * (r + 1) + 1)
                pe.wait_ge(y_half, r + 1)

            experts(0)
            pe.wait_ge(count_ready, 1)
            most = pe.value_load(cntu[0:1, 0:1])
            with pe.If(most > SLOTS):
                experts(1)
            with pe.Else():
                pe.nop()
            for i in range(4):
                t, half = divmod(i, 2)
                pe.matmul(bank[FINAL_BANK[i]][:], wselT[:, NE, P * t:P * t + P], y[:, 512 * half:512 * half + 512],
                          start=False, stop=True, skip_group_check=True).then_inc(fo_done, 1)


_OUT = ((1, 256, 1024), "float32")


def kernel(**inputs):
    import numpy as np
    import concourse.bacc as bacc
    from concourse.bass_utils import run_bass_kernel_spmd

    nc = bacc.Bacc("TRN2", target_bir_lowering=False, num_devices=1)
    names = ("x", "mem", "norm_mix_g", "w_in", "b_in", "a_conv_w", "a_conv_b", "a_ln_g", "a_ln_b", "a_w_out",
             "b_w_out", "c_conv_w", "c_w_out", "w_o", "norm_x_g", "norm_mem_g", "xq_w", "xk_w", "xv_w", "xo_w",
             "norm_ffn_g", "ffn_w1", "ffn_w3", "ffn_w2", "moe_router", "moe_w1", "moe_w3", "moe_w2", "final_g")
    arrays, args = {}, {}
    for name in names:
        a = np.ascontiguousarray(inputs[name])
        arrays[f"in_{name}"] = a
        args[name] = nc.dram_tensor(f"in_{name}", a.shape, mybir.dt.from_np(a.dtype), kind="ExternalInput").ap()
    args["out"] = nc.dram_tensor("out_0", _OUT[0], mybir.dt.from_np(np.dtype(_OUT[1])), kind="ExternalOutput").ap()
    trunk(nc, **args)
    r = run_bass_kernel_spmd(nc, [arrays], core_ids=[0])
    return r.results[0]["out_0"]
```
